# Optimizing a Trainium2 kernel written in Bass

```python
import jax, jax.numpy as jnp
from jax import lax
import numpy as np

D_MODEL = 1024
BATCH = 1
SEQ = 256
DEPTH = 2

PLE_DIM = 256
SC_WIDTH = 512
SC_CONV = 3
GLA_HEADS = 4
GLA_DK = 64
GLA_DV = 128
GLA_GATE_RANK = 16
GLA_TAU = 16.0
GLA_CHUNK = 64
MLA_HEADS = 4
MLA_NOPE = 128
MLA_ROPE = 64
MLA_V = 128
MLA_Q_RANK = 256
MLA_KV_RANK = 128
ROPE_THETA = 10000.0
Q_BLOCK = 128
N_GROUPS = 8
EXPERTS_PER_GROUP = 8
N_EXPERTS = N_GROUPS * EXPERTS_PER_GROUP
TOP_K = 2
EXPERT_HIDDEN = 256
MOE_BLOCK = 128
DN_ALPHA = (2 * DEPTH) ** 0.25
DN_BETA = (8 * DEPTH) ** -0.25
LN_EPS = 1e-5
RMS_EPS = 1e-6

GLA_QK = GLA_HEADS * GLA_DK
GLA_VW = GLA_HEADS * GLA_DV
MLA_QK = MLA_NOPE + MLA_ROPE
MLA_VW = MLA_HEADS * MLA_V
IN_SPLIT_SIZES = (SC_WIDTH, SC_WIDTH, SC_WIDTH,
                  GLA_QK, GLA_QK, GLA_VW, GLA_GATE_RANK, GLA_VW,
                  MLA_Q_RANK, MLA_KV_RANK, MLA_ROPE,
                  D_MODEL, D_MODEL, D_MODEL)
IN_WIDTH = 3 * SC_WIDTH + 2 * GLA_QK + 2 * GLA_VW + GLA_GATE_RANK + MLA_Q_RANK + MLA_KV_RANK + MLA_ROPE + 3 * D_MODEL
BR_WIDTH = SC_WIDTH + GLA_VW + MLA_VW

kernel_name = "hybrid_conv_gla_mla_hmoe_deepnorm"

def _split_points():
    pts, acc = [], 0
    for s in IN_SPLIT_SIZES[:-1]:
        acc += s
        pts.append(acc)
    return pts

def layer_norm(x, g, b):
    xf = x.astype(jnp.float32)
    mu = jnp.mean(xf, axis=-1, keepdims=True)
    xc = xf - mu
    var = jnp.mean(xc * xc, axis=-1, keepdims=True)
    return (xc * lax.rsqrt(var + LN_EPS) * g + b).astype(x.dtype)

def rms_norm(x, g):
    xf = x.astype(jnp.float32)
    return (xf * lax.rsqrt(jnp.mean(xf * xf, axis=-1, keepdims=True) + RMS_EPS) * g).astype(x.dtype)

def rope_tables(positions, dim):
    inv = 1.0 / (ROPE_THETA ** (jnp.arange(0, dim, 2, dtype=jnp.float32) / dim))
    ang = positions.astype(jnp.float32)[..., None] * inv
    return jnp.cos(ang), jnp.sin(ang)

def apply_rope(x, cos, sin):
    xf = x.astype(jnp.float32)
    x1, x2 = jnp.split(xf, 2, axis=-1)
    c, s = cos[:, :, None, :], sin[:, :, None, :]
    return jnp.concatenate([x1 * c - x2 * s, x1 * s + x2 * c], axis=-1).astype(x.dtype)

def short_gated_conv(b_gate, c_gate, xv, w_conv):
    u = c_gate * xv
    y = lax.conv_general_dilated(u, w_conv[:, None, :].astype(u.dtype), window_strides=(1,),
                                 padding=[(SC_CONV - 1, 0)],
                                 dimension_numbers=('NWC', 'WIO', 'NWC'),
                                 feature_group_count=u.shape[-1])
    return b_gate * y

def gla_chunked(q, k, v, log_a, r, norm_g):
    B, S, _ = q.shape
    C, N, H = GLA_CHUNK, S // GLA_CHUNK, GLA_HEADS
    f32 = jnp.float32
    qf = q.astype(f32).reshape(B, N, C, H, GLA_DK) * (GLA_DK ** -0.5)
    kf = k.astype(f32).reshape(B, N, C, H, GLA_DK)
    vf = v.astype(f32).reshape(B, N, C, H, GLA_DV)
    g = log_a.astype(f32).reshape(B, N, C, H, GLA_DK)
    b = jnp.cumsum(g, axis=2)
    b_last = b[:, :, -1]
    q_e = qf * jnp.exp(b)
    k_e = kf * jnp.exp(-b)
    k_t = kf * jnp.exp(b_last[:, :, None] - b)
    causal = jnp.tril(jnp.ones((C, C), dtype=bool))
    a = jnp.einsum('bnihd,bnjhd->bnhij', q_e, k_e)
    a = jnp.where(causal, a, 0.0)
    o_intra = jnp.einsum('bnhij,bnjhe->bnihe', a, vf)
    kv = jnp.einsum('bnjhd,bnjhe->bnhde', k_t, vf)
    decay = jnp.exp(b_last)

    def step(state, inp):
        kv_n, d_n = inp
        return d_n[..., None] * state + kv_n, state

    _, s_prev = lax.scan(step, jnp.zeros((B, H, GLA_DK, GLA_DV), f32),
                         (jnp.moveaxis(kv, 1, 0), jnp.moveaxis(decay, 1, 0)))
    s_prev = jnp.moveaxis(s_prev, 0, 1)
    o_inter = jnp.einsum('bnihd,bnhde->bnihe', q_e, s_prev)
    o = (o_intra + o_inter).reshape(B, S, H, GLA_DV)
    o = rms_norm(o, norm_g) * jax.nn.silu(r.astype(f32).reshape(B, S, H, GLA_DV))
    return o.reshape(B, S, GLA_VW).astype(v.dtype)

def causal_block_attention(q, k, v):
    B, S, H, Dh = q.shape
    nqb = S // Q_BLOCK
    scale = Dh ** -0.5
    qb = jnp.moveaxis(q.reshape(B, nqb, Q_BLOCK, H, Dh), 1, 0)
    k_pos = jnp.arange(S)

    def one_block(args):
        q_blk, blk = args
        s = jnp.einsum('bqhd,bkhd->bhqk', q_blk, k, preferred_element_type=jnp.float32) * scale
        q_pos = blk * Q_BLOCK + jnp.arange(Q_BLOCK)
        s = jnp.where(k_pos[None, :] <= q_pos[:, None], s, -jnp.inf)
        pr = jax.nn.softmax(s, axis=-1)
        return jnp.einsum('bhqk,bkhd->bqhd', pr.astype(v.dtype), v)

    out = lax.map(one_block, (qb, jnp.arange(nqb)))
    return jnp.moveaxis(out, 0, 1).reshape(B, S, H, v.shape[-1])

def mla(c_q, c_kv, k_rope_raw, q_norm_g, kv_norm_g, w_uq, w_ukv, cos, sin):
    B, S, _ = c_q.shape
    H = MLA_HEADS
    q = (rms_norm(c_q, q_norm_g) @ w_uq).reshape(B, S, H, MLA_QK)
    q_nope, q_rope = q[..., :MLA_NOPE], q[..., MLA_NOPE:]
    kv = (rms_norm(c_kv, kv_norm_g) @ w_ukv).reshape(B, S, H, MLA_NOPE + MLA_V)
    k_nope, v = kv[..., :MLA_NOPE], kv[..., MLA_NOPE:]
    q_rope = apply_rope(q_rope, cos, sin)
    k_rope = apply_rope(k_rope_raw[:, :, None, :], cos, sin)
    q = jnp.concatenate([q_nope, q_rope], axis=-1)
    k = jnp.concatenate([k_nope, jnp.broadcast_to(k_rope, (B, S, H, MLA_ROPE))], axis=-1)
    return causal_block_attention(q, k, v).reshape(B, S, MLA_VW)

def hier_moe(x, w_grp, b_grp, w_exp, b_exp, w_gate, w_up, w_down):
    B, S, D = x.shape
    T = B * S
    xt = x.reshape(T, D)
    grp_logits = (xt @ w_grp).astype(jnp.float32) + b_grp
    grp_prob = jax.nn.softmax(grp_logits, axis=-1)
    g_top = jnp.argmax(grp_logits, axis=-1)
    p_g = jnp.take_along_axis(grp_prob, g_top[:, None], axis=1)[:, 0]
    exp_logits = jnp.einsum('td,dge->tge', xt, w_exp).astype(jnp.float32) + b_exp
    sel = jnp.take_along_axis(exp_logits, g_top[:, None, None], axis=1)[:, 0]
    top_vals, top_idx = lax.top_k(sel, TOP_K)
    weights = p_g[:, None] * jax.nn.softmax(top_vals, axis=-1)
    expert_id = g_top[:, None] * EXPERTS_PER_GROUP + top_idx

    A = T * TOP_K
    flat_e = expert_id.reshape(A).astype(jnp.int32)
    order = jnp.argsort(flat_e)
    sorted_e = flat_e[order]
    counts = jnp.zeros((N_EXPERTS,), jnp.int32).at[flat_e].add(1)
    padded = (counts + MOE_BLOCK - 1) // MOE_BLOCK * MOE_BLOCK
    pad_end = jnp.cumsum(padded)
    pad_start = pad_end - padded
    start = jnp.cumsum(counts) - counts
    dest = pad_start[sorted_e] + jnp.arange(A, dtype=jnp.int32) - start[sorted_e]
    nb = -(-A // MOE_BLOCK) + N_EXPERTS
    row_token = jnp.full((nb * MOE_BLOCK,), T, jnp.int32).at[dest].set((order // TOP_K).astype(jnp.int32))
    block_expert = jnp.minimum(jnp.searchsorted(pad_end, jnp.arange(nb) * MOE_BLOCK, side='right'),
                               N_EXPERTS - 1)
    x_pad = jnp.concatenate([xt, jnp.zeros((1, D), xt.dtype)], axis=0)

    def run_block(args):
        tok, e = args
        xb = x_pad[tok]
        h = jax.nn.silu(xb @ w_gate[e]) * (xb @ w_up[e])
        return h @ w_down[e]

    y_rows = lax.map(run_block, (row_token.reshape(nb, MOE_BLOCK), block_expert))
    y_rows = y_rows.reshape(nb * MOE_BLOCK, D)
    y_assign = jnp.zeros((A, D), y_rows.dtype).at[order].set(y_rows[dest])
    y = jnp.sum(y_assign.reshape(T, TOP_K, D).astype(jnp.float32) * weights[..., None], axis=1)
    return y.reshape(B, S, D).astype(x.dtype)

def setup_inputs(seed: int = 0) -> dict:
    key = jax.random.key(seed)
    ks = iter(jax.random.split(key, 32))
    f32 = jnp.float32

    def nrm(shape, fan_in, scale=1.0):
        return jax.random.normal(next(ks), shape, f32) * (scale * fan_in ** -0.5)

    def gain(shape):
        return 1.0 + 0.02 * jax.random.normal(next(ks), shape, f32)

    def bias(shape):
        return 0.01 * jax.random.normal(next(ks), shape, f32)

    L = DEPTH
    return {
        "x": jax.random.normal(next(ks), (BATCH, SEQ, D_MODEL), f32),
        "p": jax.random.normal(next(ks), (DEPTH, BATCH, SEQ, PLE_DIM), f32),
        "positions": jnp.broadcast_to(jnp.arange(SEQ, dtype=jnp.int32)[None, :], (BATCH, SEQ)),
        "ln0_g": gain((D_MODEL,)),
        "ln0_b": bias((D_MODEL,)),
        "w_in": nrm((L, D_MODEL, IN_WIDTH), D_MODEL),
        "w_conv": nrm((L, SC_CONV, SC_WIDTH), SC_CONV),
        "w_gla_gate": nrm((L, GLA_GATE_RANK, GLA_QK), GLA_GATE_RANK),
        "b_gla_gate": bias((L, GLA_QK)),
        "gla_norm_g": gain((L, GLA_DV)),
        "mla_q_norm_g": gain((L, MLA_Q_RANK)),
        "mla_kv_norm_g": gain((L, MLA_KV_RANK)),
        "w_uq": nrm((L, MLA_Q_RANK, MLA_HEADS * MLA_QK), MLA_Q_RANK),
        "w_ukv": nrm((L, MLA_KV_RANK, MLA_HEADS * (MLA_NOPE + MLA_V)), MLA_KV_RANK),
        "w_br": nrm((L, BR_WIDTH, D_MODEL), SC_WIDTH, DN_BETA),
        "w_o": nrm((L, D_MODEL, D_MODEL), D_MODEL, DN_BETA),
        "ln1_g": gain((L, D_MODEL)),
        "ln1_b": bias((L, D_MODEL)),
        "w_grp": nrm((L, D_MODEL, N_GROUPS), D_MODEL),
        "b_grp": bias((L, N_GROUPS)),
        "w_exp": nrm((L, D_MODEL, N_GROUPS, EXPERTS_PER_GROUP), D_MODEL),
        "b_exp": bias((L, N_GROUPS, EXPERTS_PER_GROUP)),
        "w_gate": nrm((L, N_EXPERTS, D_MODEL, EXPERT_HIDDEN), D_MODEL),
        "w_up": nrm((L, N_EXPERTS, D_MODEL, EXPERT_HIDDEN), D_MODEL, DN_BETA),
        "w_down": nrm((L, N_EXPERTS, EXPERT_HIDDEN, D_MODEL), EXPERT_HIDDEN, DN_BETA),
        "ln2_g": gain((L, D_MODEL)),
        "ln2_b": bias((L, D_MODEL)),
        "w_ple_gate": nrm((L, D_MODEL, D_MODEL), D_MODEL),
        "b_ple_gate": bias((L, D_MODEL)),
        "w_ple_up": nrm((L, PLE_DIM, D_MODEL), PLE_DIM, DN_BETA),
        "ln3_g": gain((L, D_MODEL)),
        "ln3_b": bias((L, D_MODEL)),
    }

def reference(x, p, positions, ln0_g, ln0_b, w_in, w_conv, w_gla_gate, b_gla_gate, gla_norm_g,
              mla_q_norm_g, mla_kv_norm_g, w_uq, w_ukv, w_br, w_o, ln1_g, ln1_b,
              w_grp, b_grp, w_exp, b_exp, w_gate, w_up, w_down, ln2_g, ln2_b,
              w_ple_gate, b_ple_gate, w_ple_up, ln3_g, ln3_b):
    cos, sin = rope_tables(positions, MLA_ROPE)
    split_pts = _split_points()
    x = layer_norm(x, ln0_g, ln0_b)
    for i in range(DEPTH):
        h = x @ w_in[i]
        (a_b, a_c, a_x, gq, gk, gv, g_lr, g_r, c_q, c_kv, k_rope,
         gt_a, gt_b, gt_c) = jnp.split(h, split_pts, axis=-1)
        y_a = short_gated_conv(a_b, a_c, a_x, w_conv[i])
        log_a = jax.nn.log_sigmoid((g_lr @ w_gla_gate[i]).astype(jnp.float32) + b_gla_gate[i]) / GLA_TAU
        y_b = gla_chunked(gq, gk, gv, log_a, g_r, gla_norm_g[i])
        y_c = mla(c_q, c_kv, k_rope, mla_q_norm_g[i], mla_kv_norm_g[i],
                  w_uq[i], w_ukv[i], cos, sin)
        wb = w_br[i]
        merged = (jax.nn.sigmoid(gt_a) * (y_a @ wb[:SC_WIDTH])
                  + jax.nn.sigmoid(gt_b) * (y_b @ wb[SC_WIDTH:SC_WIDTH + GLA_VW])
                  + jax.nn.sigmoid(gt_c) * (y_c @ wb[SC_WIDTH + GLA_VW:]))
        x = layer_norm(DN_ALPHA * x + merged @ w_o[i], ln1_g[i], ln1_b[i])
        y_m = hier_moe(x, w_grp[i], b_grp[i], w_exp[i], b_exp[i], w_gate[i], w_up[i], w_down[i])
        x = layer_norm(DN_ALPHA * x + y_m, ln2_g[i], ln2_b[i])
        ple = jax.nn.sigmoid(x @ w_ple_gate[i] + b_ple_gate[i]) * (p[i] @ w_ple_up[i])
        x = layer_norm(DN_ALPHA * x + ple, ln3_g[i], ln3_b[i])
    return x


_drawn_inputs = setup_inputs


def setup_inputs(seed=0):
    import zlib

    import numpy as np

    out = dict(_drawn_inputs(seed))
    spreads = {}
    factors = {'ln0_g': 2.693,
     'ln0_b': 5.462,
     'w_gla_gate': 6.818,
     'b_gla_gate': 39.297,
     'gla_norm_g': 8.0,
     'mla_q_norm_g': 8.0,
     'mla_kv_norm_g': 8.0,
     'ln1_b': 4.051,
     'b_grp': 8.0,
     'b_exp': 8.0,
     'ln2_b': 3.942,
     'b_ple_gate': 8.0,
     'ln3_b': 3.691}
    for name, (base, spread) in spreads.items():
        noise = np.random.default_rng([zlib.crc32(name.encode()), seed]).standard_normal(out[name].shape)
        drawn = base * np.exp(spread * noise) if base else spread * noise
        out[name] = __import__('jax').numpy.asarray(drawn.astype(out[name].dtype))
    for name, factor in factors.items():
        out[name] = (out[name] * factor).astype(out[name].dtype)
    return out
```

```python
from contextlib import ExitStack

import numpy as np

import concourse.bass as bass
from concourse import mybir

F32 = mybir.dt.float32
I32 = mybir.dt.int32
U32 = mybir.dt.uint32
ALU = mybir.AluOpType
ACT = mybir.ActivationFunctionType
AX = mybir.AxisListType

D, SEQ, DEPTH, PLE = 1024, 256, 2, 256
T, K = SEQ // 128, D // 128
SC, GH, DK, DV, LR, CH = 512, 4, 64, 128, 16, 64
TAU = 16.0
MH, NOPE, ROPE, MV, QR, KVR = 4, 128, 64, 128, 256, 128
NG, EPG, NE, HID = 8, 8, 64, 256
ALPHA = float((2 * DEPTH) ** 0.25)
LN_EPS, RMS_EPS = 1e-5, 1e-6
SCALE = float((NOPE + ROPE) ** -0.5)
NLG = NG + NE

C_B, C_C, C_X = 0, SC, 2 * SC
C_QK = 3 * SC
C_V = C_QK + 2 * GH * DK
C_LR = C_V + GH * DV
C_R = C_LR + LR
C_LAT = C_R + GH * DV
LAT = QR + KVR + ROPE
C_GATE = C_LAT + LAT

RING = 12
SLOT = 2048
GROUPS = NE // 4
OVER = 16
ALLG = GROUPS + OVER // 4
ROUND = 4

JOBS = ["xT_lo", "xT_hi", "vecT", "lat", "gqk", "glr", "z", "latT", "krT", "gv", "qn", "qr", "kn", "vv",
        "ktT", "ab", "qrT", "AT", "sc0", "kv0", "kv2", "sc1", "ac", "gr", "pT0", "pT1", "glao", "ax",
        "yc", "ybT"]
BRANCHES = ("a", "c", "b")
BROW = {"a": 0, "b": 1, "c": 2}
for _b in BRANCHES:
    for _h in range(2):
        JOBS += [f"gate_{_b}{_h}", f"br_{_b}{_h}"]
JOBS += ["wo0", "wo1", "x1T_lo", "x1T_hi", "logit", "rank", "x2T_lo", "x2T_hi", "pTr", "pg0", "pg1", "pu0", "pu1"]
JOBS_OF = [len(JOBS[p::4]) for p in range(4)]

UNITS = ["lat0", "lat1", "gqk0", "gqk1", "gv0", "gv1", "uq", "ukv", "ab0", "ab1", "ac0", "ac1", "gr0", "gr1",
         "ax0", "ax1"]
for _b in BRANCHES:
    for _h in range(2):
        UNITS += [f"gate_{_b}{_h}0", f"gate_{_b}{_h}1", f"wbr_{_b}{_h}"]
UNITS += ["wo_0", "wo_1", "wo_2", "wo_3", "ln1"]
MOE0 = len(UNITS)
MOE_UNITS = ALLG * 12
TAIL = ["ln2", "pgw0", "pgw1", "pgw2", "pgw3", "p", "pup", "bple", "ln3"]
TAIL0 = MOE0 + MOE_UNITS
PER_LAYER = TAIL0 + len(TAIL)
assert PER_LAYER % RING == 0, PER_LAYER
TURNS = PER_LAYER // RING
SMALL_LOADS = 11
CARRIED = 3

DVE_CHAIN = (14, 55, 4, 1)
ACT_CHAIN = (0, 1, 0, 0)



def build(nc, a):
    ctx = ExitStack()
    with ctx:
        def sb(name, shape, dt=F32):
            return ctx.enter_context(nc.sbuf_tensor(name, shape, dt))

        def sem(name):
            return ctx.enter_context(nc.semaphore(name))

        ring = sb("ring", [128, RING, SLOT])
        x = sb("x", [128, T, D])
        xT = sb("xT", [128, K, SEQ])
        ident = sb("ident", [128, 128])
        gmask = sb("gmask", [128, 128], I32)
        smask = sb("smask", [128, 128])
        tri = sb("tri", [128, 128])
        ones = sb("ones", [128, 128])
        iota = sb("iota", [128, NE])
        iota32m = sb("iota32m", [128, 7])
        inv = sb("inv", [128, ROPE // 2])
        cos = sb("cos", [128, T, ROPE // 2])
        sin = sb("sin", [128, T, ROPE // 2])
        qpad = sb("qpad", [128, GH, SEQ])
        ATm = sb("ATm", [128, T, GH, 128])
        krp = sb("krp", [128, T, 2, 128])
        wlr = sb("wlr", [128, K, LR])
        wgg = sb("wgg", [LR, GH * DK])
        gnorm = sb("gnorm", [128, DV])
        vec = sb("vec", [17, 128])
        vecT = sb("vecT", [128, 17])
        wr = sb("wr", [128, K, NLG])
        br = sb("br", [128, NLG])
        st = sb("st", [128, 64])
        posi = sb("posi", [128, T], I32)
        posf = sb("posf", [128, T])
        minus_half = sb("minus_half", [128, 8])
        st6 = sb("st6", [128, T, 2, 6])
        mv = sb("mv", [128, T, 2])
        rstd = sb("rstd", [128, T])

        NS = 19592
        S = sb("scratch", [128, NS])
        used = [0]

        def area(n):
            o = used[0]
            used[0] += n
            assert used[0] <= NS, used[0]
            return o

        def v2(o, *dims):
            n = int(np.prod(dims))
            ap = S[:, o:o + n]
            if len(dims) == 1:
                return ap
            if len(dims) == 2:
                return ap.rearrange("p (a b) -> p a b", a=dims[0])
            if len(dims) == 3:
                return ap.rearrange("p (a b c) -> p a b c", a=dims[0], b=dims[1])

        oM = area(4096)
        merged = v2(oM, K, SEQ)
        sig = [v2(oM + 2048, 4, SEQ), v2(oM + 3072, 4, SEQ)]
        qk = v2(oM, 4, SEQ)
        zb = v2(oM + 1024, 2, SEQ)
        za = v2(oM + 1536, 2, SEQ)
        bcum = v2(oM + 2048, 2, SEQ)
        E3 = v2(oM + 2560, 2, SEQ)
        ktF = v2(oM + 3072, 2, SEQ)
        ke = v2(oM + 3584, 2, SEQ)
        oE = area(1024)
        E1 = v2(oE, 2, SEQ)
        E2 = v2(oE + 512, 2, SEQ)
        kt = v2(area(512), T, 2, 128)
        vg = v2(area(1024), T, 512)
        rs = v2(area(1024), T, GH, DV)
        St = v2(area(1536), 3, 2, 256)
        oL = area(896 + 512 + 256)
        lat = v2(oL, T, LAT)
        cqT = v2(oL + 896, 2, SEQ)
        ckvT = v2(oL + 896 + 512, SEQ)
        pT0 = v2(oL, MH, SEQ)
        pT1 = v2(oL + 1024, MH, 128)
        krT = v2(area(512), 2, SEQ)
        oQ = area(1024)
        qnT = v2(oQ, MH, SEQ)
        ycT = v2(oQ, MH, SEQ)
        qrT = v2(area(512), 2, SEQ)
        oK = area(1024)
        knT = v2(oK, MH, SEQ)
        ybT = v2(oK, GH, SEQ)
        vm = v2(area(1024), T, 512)
        oS = area(1536)
        sc0 = v2(oS, MH, 128)
        sc1 = v2(oS + 512, MH, SEQ)
        qr = v2(oS, T, MH, ROPE)
        rope_tmp = [v2(oS + 512 + 256 * i, T, MH, ROPE // 2) for i in range(4)]
        yaT = v2(area(1024), 4, SEQ)
        ac = v2(area(1024), 4, SEQ)
        u = v2(area(4 * (SEQ + 2)), 4, SEQ + 2)
        yT = {"a": yaT, "b": ybT, "c": ycT}
        junk = v2(oE, 8, 128)
        glrT = za[0:LR, 0, :]
        gmask_f = qk[:, 0, 0:128]
        used[0] = 0
        xp = v2(area(2048), T, K, 128)
        yacc = v2(area(2048), T, D)
        Psel = [v2(area(256), T, 128) for _ in range(2)]
        Pw = [v2(area(256), T, 128) for _ in range(2)]
        xgT = v2(area(1024), K, 128)
        silu = v2(area(256), 256)
        hperm = v2(area(256), 2, 128)
        hT = v2(area(256), 2, 128)
        PwT = v2(area(256), 256)
        ysb = v2(area(1024), D)
        NR = 4 * (ALLG + 1)
        rankx = v2(area(T * NR), T, NR)
        wx = v2(area(T * NR), T, NR)
        asg = v2(area(T * NE), T, NE)
        lg = v2(area(T * NLG), T, NLG)
        rt = v2(area(T * 64), T, 64)
        nov = v2(area(NE), NE)
        cum = v2(area(NE), NE)
        big = [v2(area(OVER * NE), OVER, NE) for _ in range(3)]
        ov = v2(area(4 * OVER), 4, OVER)
        cnt = v2(area(NE), NE)
        oe = sb("oe", [128, OVER + 1], I32)
        idx = sb("idx", [128, 4, 8], U32)
        used[0] = 4096
        pT = v2(area(512), 2, SEQ)
        pgs = v2(area(2048), 2, T, 512)
        ln0gb = v2(area(2048), 2, D)

        ps = ctx.enter_context(nc.psum_tensor("ps", [128, 8, 512], F32))

        full = [sem(f"job_full{p}") for p in range(4)]
        free = [sem(f"job_free{p}") for p in range(4)]
        landed = [sem(f"landed{i}") for i in range(RING)]
        ring_free = sem("ring_free")
        x_ready = sem("x_ready")
        small = sem("small_loads")
        pre = sem("first_loads")
        consts = sem("consts")
        dve_chain, act_chain = sem("dve_chain"), sem("act_chain")
        pool_chain = sem("pool_chain")
        ev = {n: sem(n) for n in (
            "lat_squares lat_normed kr_ready zabs_ready lnz_ready "
            "bcum_ready exps_ready gla_in_ready ktF_ready qr_ready "
            "ya_ready max0_ready exp0_ready "
            "soft0_ready max1_ready exp1_ready soft1_ready o_squares "
            "xp_ready gmax_ready gexp_ready dtop_ready etop_ready asg_ready over_ready "
            "yacc_zero cs_ready ang_ready").split()}
        sig_used, pgs_sig = sem("sig_used"), sem("ple_sigmoid")
        P_ready, gathered, xg_a, xg_d = sem("P_ready"), sem("gathered"), sem("xg_by_act"), sem("xg_by_dve")
        pwt_full, pwt_ready = sem("pwt_full"), sem("pwt_ready")
        h_full, silu_ready, h_ready = sem("h_full"), sem("silu_ready"), sem("h_ready")
        ht_full, ht_ready = sem("ht_full"), sem("ht_ready")
        y_full, y_ready = sem("y_full"), sem("y_ready")
        c_full, acc_done = sem("c_full"), sem("acc_done")
        out_done = sem("out_done")
        passed = sem("waits_passed")
        power_in, power_out = sem("power_in"), sem("power_out")
        eps_added = sem("eps_added")

        def bank(p, i=0):
            return 2 * (p % 4) + i

        def job(name):
            n = JOBS.index(name)
            return n % 4, n // 4

        def pair(name):
            p = job(name)[0]
            return ps[:, 2 * p:2 * p + 2, :].rearrange("p a b -> p (a b)")

        def half(name, i):
            return ps[:, 2 * job(name)[0] + i, :]

        def wait_full(eng, name, L):
            p, i = job(name)
            eng.wait_ge(full[p], L * JOBS_OF[p] + (i + 1))

        def wait_free(eng, name, L):
            p, i = job(name)
            eng.wait_ge(free[p], L * JOBS_OF[p] + (i + 1))

        def wait_read(eng, name, L):
            p, i = job(name)
            eng.wait_ge(free[p], L * JOBS_OF[p] + (i + 2))
            alone(eng)

        def unit_pos(name):
            return UNITS.index(name) if name in UNITS else TAIL0 + TAIL.index(name)

        def unit(name):
            return ring[:, unit_pos(name) % RING, :]

        def wait_unit(eng, name, L):
            q = unit_pos(name)
            eng.wait_ge(landed[q % RING], L * (16 * TURNS) + 16 * (q // RING + 1))

        def once(eng, name, L):
            eng.wait_ge(ev[name], L + 1)

        def alone(eng):
            eng.sem_inc(passed, 1)

        class Chain:

            def __init__(self, eng, s, expected):
                self.eng, self.s, self.exp = eng, s, expected
                self.base, self.c = 0, 0
                self.per = expected[1] + (GROUPS // ROUND) * expected[2] + (ALLG - GROUPS) * expected[3]

            def link(self, ins):
                self.c += 1
                ins.then_inc(self.s, 1)
                self.eng.wait_ge(self.s, self.base + self.c)

            def check(self, i):
                assert self.c == self.exp[i], (self.s, i, self.c)

        block = ctx.enter_context(nc.Block())

        @block.sync
        def _(sp):
            def issue(q, L, src, dst):
                sp.wait_ge(ring_free, L * PER_LAYER + (q + 1))
                alone(sp)
                sp.dma_start(dst, src).then_inc(landed[q % RING], 16)

            def w_rows(w, L, r0, nk, c0, nc_):
                return w[bass.ds(L, 1), r0:r0 + 128 * nk, c0:c0 + nc_].rearrange("l (k p) n -> p (l k) n", p=128)

            def rows_unit(q, L, w, r0, nk, c0, nc_):
                dst = ring[:, q % RING, 0:nk * nc_].rearrange("p (k n) -> p k n", k=nk)
                issue(q, L, w_rows(w, L, r0, nk, c0, nc_), dst)

            starts = {"gqk": C_QK, "gv": C_V, "ab": C_B, "ac": C_C, "ax": C_X, "gr": C_R}
            with sp.Fori(0, DEPTH) as L:
                for q, name in enumerate(UNITS):
                    if name in ("lat0", "lat1"):
                        rows_unit(q, L, a["w_in"], 512 * int(name[-1]), 4, C_LAT, LAT)
                    elif name[:-1] in starts:
                        rows_unit(q, L, a["w_in"], 512 * int(name[-1]), 4, starts[name[:-1]], 512)
                    elif name == "uq":
                        rows_unit(q, L, a["w_uq"], 0, 2, 0, MH * (NOPE + ROPE))
                    elif name == "ukv":
                        rows_unit(q, L, a["w_ukv"], 0, 1, 0, MH * (NOPE + MV))
                    elif name.startswith("gate_"):
                        c0 = C_GATE + D * BROW[name[5]] + 512 * int(name[6])
                        rows_unit(q, L, a["w_in"], 512 * int(name[7]), 4, c0, 512)
                    elif name.startswith("wbr_"):
                        rows_unit(q, L, a["w_br"], 512 * BROW[name[4]], 4, 512 * int(name[5]), 512)
                    elif name.startswith("wo_"):
                        rows_unit(q, L, a["w_o"], 256 * int(name[3]), 2, 0, D)
                    elif name == "ln1":
                        issue(q, L, a["ln1"][bass.ds(L, 1), :, :].rearrange("l g d -> l (g d)")
                              .to_broadcast([128, 2 * D]), ring[:, q % RING, :])
                    else:
                        raise ValueError(name)

                def load_group(base, experts):
                    n = 0
                    for j in range(4):
                        for w in (a["w_gate"], a["w_up"]):
                            q = MOE0 + n
                            sp.wait_ge(ring_free, base + (MOE0 + n + 1))
                            alone(sp)
                            sp.dma_start(ring[:, q % RING, :],
                                         w[bass.ds(experts[j], 1), :, :].rearrange("e (p k) n -> p (e k n)", k=K)
                                         ).then_inc(landed[q % RING], 16)
                            n += 1
                    for j in range(4):
                        q = MOE0 + n
                        sp.wait_ge(ring_free, base + (MOE0 + n + 1))
                        alone(sp)
                        sp.dma_start(ring[:, q % RING, :],
                                     a["w_down"][bass.ds(experts[j], 1), :, :].rearrange("e (p c) n -> p (e c n)", c=2)
                                     ).then_inc(landed[q % RING], 16)
                        n += 1

                with sp.Fori(0, GROUPS) as s:
                    load_group(L * PER_LAYER + s * 12, [L * NE + s * 4 + j for j in range(4)])
                once(sp, "over_ready", L)
                alone(sp)
                n_over = sp.value_load(oe[0:1, OVER:OVER + 1], min_val=0, max_val=OVER)
                with sp.If(n_over > 0):
                    with sp.Fori(0, OVER // 4) as g:
                        es = [sp.value_load(oe[0:1, bass.ds(g * 4 + j, 1)], min_val=0, max_val=NE - 1)
                              for j in range(4)]
                        load_group(L * PER_LAYER + g * 12 + GROUPS * 12, [L * NE + e for e in es])
                with sp.Else():
                    for i in range(RING):
                        q = MOE0 + 12 * (GROUPS - 1) + i
                        sp.wait_ge(landed[q % RING], L * (16 * TURNS) + 16 * (q // RING + 1))
                        alone(sp)
                    for i in range(RING):
                        sp.sem_inc(landed[i], 16 * (ALLG - GROUPS))
                for i, name in enumerate(TAIL):
                    q = TAIL0 + i
                    if name in ("ln2", "ln3"):
                        issue(q, L, a[name][bass.ds(L, 1), :, :].rearrange("l g d -> l (g d)")
                              .to_broadcast([128, 2 * D]), ring[:, q % RING, :])
                    elif name.startswith("pgw"):
                        rows_unit(q, L, a["w_ple_gate"], 256 * int(name[3]), 2, 0, D)
                    elif name == "p":
                        rows_unit(q, L, a["p"], 0, T, 0, PLE)
                    elif name == "pup":
                        rows_unit(q, L, a["w_ple_up"], 0, 2, 0, D)
                    elif name == "bple":
                        issue(q, L, a["b_ple_gate"][bass.ds(L, 1), :].to_broadcast([128, D]), ring[:, q % RING, 0:D])
            for t in range(T):
                sp.wait_ge(x_ready, 3 * DEPTH + 2)
                sp.dma_start(a["out"][0, 128 * t:128 * t + 128, :], x[:, t, :]).then_inc(out_done, 16)
            sp.wait_ge(out_done, 16 * T)

        @block.gpsimd
        def _(pool):
            pool.dma_start(x[:, :, :], a["x"][0].rearrange("(t p) d -> p t d", p=128)).then_inc(pre, 16)
            pool.dma_start(ln0gb, a["ln0"].rearrange("g d -> (g d)").unsqueeze(0).to_broadcast([128, 2 * D])
                           .rearrange("p (g d) -> p g d", g=2)).then_inc(pre, 16)
            pool.dma_start(posi[:, :], a["positions"][0].rearrange("(t p) -> p t", p=128),
                           allow_slow_non_contiguous=True).then_inc(pre, 16)
            pool.memset(st[:, 62:63], 0.0).then_inc(ring_free, RING - CARRIED)
            for sm in (*free, x_ready, acc_done):
                pool.sem_inc(sm, 1)
            n = 0

            def c(ins):
                nonlocal n
                n += 1
                ins.then_inc(pool_chain, 1)
                pool.wait_ge(pool_chain, n)

            pool.memset(ident[:, :], 0.0)
            pool.memset(gmask_f[:, :], 1.0)
            pool.memset(smask[:, :], 0.0)
            pool.memset(ones[:, :], 1.0)
            pool.memset(tri[:, :], 1.0)
            pool.memset(qpad[:, :, :], 0.0)
            pool.memset(minus_half[:, :], -0.5)
            pool.memset(ATm[:, :, :, :], 0.0)
            for i in range(ROPE // 2):
                pool.memset(inv[:, i:i + 1], float(np.float32(1.0) / np.float32(10000.0) ** (np.float32(2 * i) / np.float32(ROPE))))
            c(pool.memset(krp[:, :, :, :], 0.0))
            pool.affine_select(out=ident[:, :], in_=ident[:, :], compare_op=ALU.not_equal, fill=1.0, base=0,
                               pattern=[[-1, 128]], channel_multiplier=1)
            pool.affine_select(out=gmask_f[:, :], in_=gmask_f[:, :], compare_op=ALU.is_ge, fill=0.0, base=0,
                               pattern=[[1, 128]], channel_multiplier=-1)
            pool.affine_select(out=smask[:, :], in_=smask[:, :], compare_op=ALU.is_ge, fill=-1e30, base=0,
                               pattern=[[-1, 128]], channel_multiplier=1)
            pool.affine_select(out=tri[:, :], in_=tri[:, :], compare_op=ALU.is_gt, fill=0.0, base=0,
                               pattern=[[1, 128]], channel_multiplier=-1)
            pool.iota(iota[:, :], [[1, NE]], base=0, channel_multiplier=0, allow_small_or_imprecise_dtypes=True)
            c(pool.iota(iota32m[:, :], [[32, 7]], base=32, channel_multiplier=0, allow_small_or_imprecise_dtypes=True))
            c(pool.memset(gmask_f[0:64, 64:128], 0.0))
            c(pool.tensor_copy(gmask[:, :], gmask_f[:, :]))
            pool.memset(st[:, 63:64], 0.0).then_inc(consts, 1)
            def rsqrt(out, ms, eps, n):
                pool.tensor_scalar(out, ms, eps, None, ALU.add).then_inc(eps_added, 1)
                pool.wait_ge(eps_added, n)
                pool.tensor_tensor(out, out, minus_half[:, 0:out.shape[1]], ALU.pow).then_inc(power_out, 1)

            pool.wait_ge(power_in, 1)
            rsqrt(rstd[:, :], mv[:, :, 1], LN_EPS, 1)
            with pool.Fori(0, DEPTH) as L:
                pool.wait_ge(x_ready, 3 * L + 1)
                pool.dma_start(wlr[:, :, :], a["w_in"][bass.ds(L, 1), :, C_LR:C_LR + LR]
                               .rearrange("l (k p) n -> p (l k) n", p=128)).then_inc(small, 16)
                pool.dma_start(wgg[:, :], a["w_gla_gate"][bass.ds(L, 1), :, :].rearrange("l r n -> (l r) n")).then_inc(small, 16)
                pool.dma_start(gnorm[:, :], a["gla_norm_g"][bass.ds(L, 1), :].to_broadcast([128, DV])).then_inc(small, 16)
                pool.dma_start(vec[0:12, :], a["w_conv"][bass.ds(L, 1), :, :].rearrange("l k (t p) -> (l k t) p", p=128)).then_inc(small, 16)
                pool.dma_start(vec[12:14, :], a["b_gla_gate"][bass.ds(L, 1), :].rearrange("l (t p) -> (l t) p", p=128)).then_inc(small, 16)
                pool.dma_start(vec[14:16, :], a["mla_q_norm_g"][bass.ds(L, 1), :].rearrange("l (t p) -> (l t) p", p=128)).then_inc(small, 16)
                pool.dma_start(vec[16:17, :], a["mla_kv_norm_g"][bass.ds(L, 1), :]).then_inc(small, 16)
                pool.dma_start(wr[:, :, 0:NG], a["w_grp"][bass.ds(L, 1), :, :].rearrange("l (k p) n -> p (l k) n", p=128)).then_inc(small, 16)
                pool.dma_start(wr[:, :, NG:NLG], a["w_exp"][bass.ds(L, 1), :, :].rearrange("l (k p) n -> p (l k) n", p=128)).then_inc(small, 16)
                pool.dma_start(br[:, 0:NG], a["b_grp"][bass.ds(L, 1), :].to_broadcast([128, NG])).then_inc(small, 16)
                pool.dma_start(br[:, NG:NLG], a["b_exp"][bass.ds(L, 1), :].to_broadcast([128, NE])).then_inc(small, 16)
                once(pool, "lat_squares", L)
                alone(pool)
                rsqrt(st[:, 4:8], st[:, 0:4], RMS_EPS, 5 * L + 2)
                once(pool, "o_squares", L)
                alone(pool)
                rsqrt(st[:, 40:48], st[:, 40:48], RMS_EPS, 5 * L + 3)
                for i in range(3):
                    pool.wait_ge(power_in, 3 * L + (i + 2))
                    alone(pool)
                    rsqrt(rstd[:, :], mv[:, :, 1], LN_EPS, 5 * L + (i + 4))

        @block.tensor
        def _(pe):
            mm = pe.matmul

            def start_job(name, L):
                wait_free(pe, name, L)

            def end_job(name, ins):
                ins.then_inc(full[job(name)[0]], 1)

            def fm(name, units, L, nk=K, rhs=None, m_of=None):
                for un in units:
                    wait_unit(pe, un, L)
                start_job(name, L)
                per = nk // len(units)
                w = [unit(un).rearrange("p (k n) -> p k n", k=per) for un in units]
                out = pair(name)
                for m in range(4):
                    for k in range(nk):
                        ins = mm(out[:, m * SEQ:m * SEQ + SEQ], w[k // per][:, k % per, m * 128:m * 128 + 128],
                                 rhs[:, k, :], start=(k == 0), stop=(k == nk - 1))
                        if m == 0 and k == 0:
                            flush(ins)
                end_job(name, ins)
                pe_release(len(units))

            def tm(name, units, L, ncols):
                for un in units:
                    wait_unit(pe, un, L)
                start_job(name, L)
                w = [unit(un)[:, 0:4 * ncols].rearrange("p (k n) -> p k n", k=4) for un in units]
                for t in range(T):
                    for k in range(K):
                        ins = mm(half(name, t)[:, 0:ncols], xT[:, k, 128 * t:128 * t + 128], w[k // 4][:, k % 4, :],
                                 start=(k == 0), stop=(k == K - 1))
                        if t == 0 and k == 0:
                            flush(ins)
                end_job(name, ins)
                pe_release(len(units))

            pending = [0]

            def pe_release(n):
                pending[0] += n

            def flush(ins):
                if pending[0]:
                    ins.then_inc(ring_free, pending[0])
                    pending[0] = 0

            def transposes_of_x(lo, hi, rnd, L):
                pe.wait_ge(x_ready, 3 * L + (rnd + 2))
                for n, name in enumerate((lo, hi)):
                    start_job(name, L)
                    for kk in range(4):
                        k = 4 * n + kk
                        for t in range(T):
                            o = kk * SEQ + t * 128
                            ins = pe.transpose(pair(name)[:, o:o + 128], x[:, t, k * 128:k * 128 + 128], ident[:, :])
                            if kk == 0 and t == 0:
                                flush(ins)
                    end_job(name, ins)

            def wait_xT(rnd, L):
                for part in ("lo", "hi"):
                    wait_read(pe, ("xT_", "x1T_", "x2T_")[rnd] + part, L)

            pe.wait_ge(consts, 1)
            with pe.Fori(0, DEPTH) as L:
                pending[0] = CARRIED
                transposes_of_x("xT_lo", "xT_hi", 0, L)
                pe.wait_ge(small, L * (16 * SMALL_LOADS) + 16 * SMALL_LOADS)
                start_job("vecT", L)
                alone(pe)
                end_job("vecT", pe.transpose(pair("vecT")[:, 0:17], vec[:, :], ident[0:17, 0:17]))
                wait_xT(0, L)
                tm("lat", ("lat0", "lat1"), L, LAT)
                fm("gqk", ("gqk0", "gqk1"), L, rhs=xT)

                start_job("glr", L)
                for k in range(K):
                    ins = mm(pair("glr")[0:LR, 0:SEQ], wlr[:, k, :], xT[:, k, :], start=(k == 0), stop=(k == K - 1))
                    if k == 0:
                        flush(ins)
                end_job("glr", ins)

                wait_read(pe, "glr", L)
                start_job("z", L)
                for i in range(2):
                    ins = mm(pair("z")[:, i * SEQ:i * SEQ + SEQ], wgg[:, i * 128:i * 128 + 128], glrT,
                             start=True, stop=True)
                end_job("z", ins)

                once(pe, "lat_normed", L)
                start_job("latT", L)
                for i in range(3):
                    for t in range(T):
                        o = i * SEQ + t * 128
                        ins = pe.transpose(pair("latT")[:, o:o + 128], lat[:, t, i * 128:i * 128 + 128], ident[:, :])
                end_job("latT", ins)
                once(pe, "kr_ready", L)
                start_job("krT", L)
                for i in range(2):
                    for t in range(T):
                        o = i * SEQ + t * 128
                        ins = pe.transpose(pair("krT")[:, o:o + 128], krp[:, t, i, :], ident[:, :])
                end_job("krT", ins)

                tm("gv", ("gv0", "gv1"), L, 512)

                wait_read(pe, "latT", L)
                wait_unit(pe, "uq", L)
                start_job("qn", L)
                wuq = unit("uq")[:, 0:2 * MH * (NOPE + ROPE)].rearrange("p (k h n) -> p k h n", k=2, h=MH)
                first = True
                for h in range(MH):
                    for k in range(2):
                        ins = mm(pair("qn")[:, h * SEQ:h * SEQ + SEQ], wuq[:, k, h, 0:NOPE], cqT[:, k, :],
                                 start=(k == 0), stop=(k == 1))
                        if first:
                            flush(ins)
                            first = False
                end_job("qn", ins)
                start_job("qr", L)
                for t in range(T):
                    for k in range(2):
                        ins = mm(half("qr", t)[:, 0:MH * ROPE], cqT[:, k, 128 * t:128 * t + 128],
                                 wuq[:, k, :, NOPE:NOPE + ROPE], start=(k == 0), stop=(k == 1))
                end_job("qr", ins)
                wait_unit(pe, "ukv", L)
                wukv = unit("ukv")[:, 0:MH * (NOPE + MV)].rearrange("p (h n) -> p h n", h=MH)
                start_job("kn", L)
                for h in range(MH):
                    ins = mm(pair("kn")[:, h * SEQ:h * SEQ + SEQ], wukv[:, h, 0:NOPE], ckvT, start=True, stop=True)
                end_job("kn", ins)
                start_job("vv", L)
                for t in range(T):
                    ins = mm(half("vv", t), ckvT[:, 128 * t:128 * t + 128], wukv[:, :, NOPE:NOPE + MV],
                             start=True, stop=True)
                end_job("vv", ins)
                pe_release(2)

                once(pe, "ktF_ready", L)
                start_job("ktT", L)
                for t in range(T):
                    for i in range(2):
                        o = (t * 2 + i) * 128
                        ins = pe.transpose(pair("ktT")[:, o:o + 128], ktF[:, i, 128 * t:128 * t + 128], ident[:, :])
                        if t == 0 and i == 0:
                            flush(ins)
                end_job("ktT", ins)

                fm("ab", ("ab0", "ab1"), L, rhs=xT)

                once(pe, "qr_ready", L)
                start_job("qrT", L)
                for i in range(2):
                    for t in range(T):
                        o = i * SEQ + t * 128
                        ins = pe.transpose(pair("qrT")[:, o:o + 128],
                                           qr[:, t, 2 * i:2 * i + 2, :].rearrange("p h n -> p (h n)"), ident[:, :])
                        if i == 0 and t == 0:
                            flush(ins)
                end_job("qrT", ins)

                once(pe, "gla_in_ready", L)
                start_job("AT", L)
                for t in range(T):
                    for h in range(GH):
                        o = (t * GH + h) * 128
                        ins = mm(pair("AT")[:, o:o + 128], ke[:, h // 2, 128 * t:128 * t + 128],
                                 qpad[:, h, 128 * t:128 * t + 128], start=True, stop=True)
                end_job("AT", ins)

                def scores(name, t, nkeys):
                    start_job(name, L)
                    for h in range(MH):
                        o = h * nkeys
                        mm(pair(name)[:, o:o + nkeys], qnT[:, h, 128 * t:128 * t + 128], knT[:, h, 0:nkeys],
                           start=True, stop=False)
                        ins = mm(pair(name)[:, o:o + nkeys], qrT[:, h // 2, 128 * t:128 * t + 128],
                                 krT[:, h % 2, 0:nkeys], start=False, stop=True)
                    end_job(name, ins)

                for n in ("qn", "kn", "qrT", "krT"):
                    wait_read(pe, n, L)
                scores("sc0", 0, 128)

                wait_read(pe, "ktT", L)
                wait_read(pe, "gv", L)

                def increments(name, chunks):
                    start_job(name, L)
                    for c in chunks:
                        p0, t = 64 * (c % 2), c // 2
                        for i in range(2):
                            ins = mm(half(name, c % 2)[:, i * 256:i * 256 + 256], kt[p0:p0 + 64, t, i, :],
                                     vg[p0:p0 + 64, t, i * 256:i * 256 + 256], start=True, stop=True)
                    end_job(name, ins)

                increments("kv0", (0, 1))
                increments("kv2", (2,))
                scores("sc1", 1, SEQ)

                fm("ac", ("ac0", "ac1"), L, rhs=xT)
                tm("gr", ("gr0", "gr1"), L, 512)

                once(pe, "soft0_ready", L)
                once(pe, "soft1_ready", L)
                start_job("pT0", L)
                for h in range(MH):
                    ins = pe.transpose(pair("pT0")[:, h * SEQ:h * SEQ + 128], sc0[:, h, :], ident[:, :])
                    if h == 0:
                        flush(ins)
                    ins = pe.transpose(pair("pT0")[:, h * SEQ + 128:h * SEQ + 256], sc1[:, h, 0:128], ident[:, :])
                end_job("pT0", ins)
                start_job("pT1", L)
                for h in range(MH):
                    ins = pe.transpose(pair("pT1")[:, h * 128:h * 128 + 128], sc1[:, h, 128:256], ident[:, :])
                end_job("pT1", ins)

                wait_read(pe, "AT", L)
                wait_read(pe, "kv2", L)
                start_job("glao", L)
                for t in range(T):
                    for h in range(GH):
                        o = half("glao", t)[:, h * 128:h * 128 + 128]
                        ins = mm(o, ATm[:, t, h, :], vg[:, t, h * 128:h * 128 + 128], start=True, stop=True,
                                 skip_group_check=True)
                        for cc in range(2):
                            c = 2 * t + cc
                            if c:
                                ins = mm(o[64 * cc:64 * cc + 64, :], qpad[:, h, 64 * c:64 * c + 64],
                                         St[:, c - 1, h // 2, (h % 2) * 128:(h % 2) * 128 + 128],
                                         start=False, stop=True, skip_group_check=True)
                end_job("glao", ins)

                fm("ax", ("ax0", "ax1"), L, rhs=xT)

                wait_read(pe, "pT0", L)
                wait_read(pe, "pT1", L)
                wait_read(pe, "vv", L)
                start_job("yc", L)
                for h in range(MH):
                    o = h * SEQ
                    ins = mm(pair("yc")[:, o:o + SEQ], vm[:, 0, h * 128:h * 128 + 128], pT0[:, h, :],
                             start=True, stop=True, skip_group_check=True)
                    if h == 0:
                        flush(ins)
                    ins = mm(pair("yc")[:, o + 128:o + 256], vm[:, 1, h * 128:h * 128 + 128], pT1[:, h, :],
                             start=False, stop=True, skip_group_check=True)
                end_job("yc", ins)

                wait_read(pe, "glao", L)
                start_job("ybT", L)
                for h in range(GH):
                    for t in range(T):
                        o = h * SEQ + t * 128
                        ins = pe.transpose(pair("ybT")[:, o:o + 128], rs[:, t, h, :], ident[:, :])
                end_job("ybT", ins)

                for b in BRANCHES:
                    for h in range(2):
                        fm(f"gate_{b}{h}", (f"gate_{b}{h}0", f"gate_{b}{h}1"), L, rhs=xT)
                        if h == 0 and b == "a":
                            once(pe, "ya_ready", L)
                        elif h == 0:
                            wait_read(pe, {"b": "ybT", "c": "yc"}[b], L)
                        name, un = f"br_{b}{h}", f"wbr_{b}{h}"
                        wait_unit(pe, un, L)
                        start_job(name, L)
                        w = unit(un).rearrange("p (k n) -> p k n", k=4)
                        for m in range(4):
                            for k in range(4):
                                ins = mm(pair(name)[:, m * SEQ:m * SEQ + SEQ], w[:, k, m * 128:m * 128 + 128],
                                         yT[b][:, k, :], start=(k == 0), stop=(k == 3))
                                if m == 0 and k == 0:
                                    flush(ins)
                        end_job(name, ins)
                        pe_release(1)

                def tm_pair(jobs, unit_names, lhsT, rhs_of):
                    for n in jobs:
                        start_job(n, L)
                    nk = 2 * len(unit_names)
                    for i, un in enumerate(unit_names):
                        wait_unit(pe, un, L)
                        w = unit(un).rearrange("p (k n) -> p k n", k=2)
                        for kk in range(2):
                            k = 2 * i + kk
                            for n in range(2):
                                for t in range(T):
                                    ins = mm(half(jobs[n], t), lhsT[:, k, 128 * t:128 * t + 128],
                                             w[:, kk, n * 512:n * 512 + 512], start=(k == 0), stop=(k == nk - 1))
                                    if kk == 0 and n == 0 and t == 0:
                                        flush(ins)
                                    if k == nk - 1 and t == T - 1:
                                        end_job(jobs[n], ins)
                        pe_release(1)

                pe.wait_ge(sig_used, 4 * L + 4)
                tm_pair(("wo0", "wo1"), [f"wo_{i}" for i in range(4)], merged, None)

                pe_release(1)
                transposes_of_x("x1T_lo", "x1T_hi", 1, L)
                wait_xT(1, L)
                start_job("logit", L)
                for t in range(T):
                    for k in range(K):
                        ins = mm(half("logit", t)[:, 0:NLG], xT[:, k, 128 * t:128 * t + 128], wr[:, k, :],
                                 start=(k == 0), stop=(k == K - 1))
                end_job("logit", ins)
                once(pe, "asg_ready", L)
                start_job("rank", L)
                r = half("rank", 0)
                mm(r[:, 0:NE], tri[:, :], asg[:, 0, :], start=True, stop=True)
                mm(r[:, NE:2 * NE], tri[:, :], asg[:, 1, :], start=True, stop=False)
                mm(r[:, NE:2 * NE], ones[:, :], asg[:, 0, :], start=False, stop=True)
                mm(r[:, 2 * NE:3 * NE], ones[:, :], asg[:, 0, :], start=True, stop=False)
                ins = mm(r[:, 2 * NE:3 * NE], ones[:, :], asg[:, 1, :], start=False, stop=True)
                end_job("rank", ins)

                for p in range(4):
                    n = len([j for j in range(JOBS.index("rank") + 1) if j % 4 == p])
                    pe.wait_ge(free[p], L * JOBS_OF[p] + (n + 1))
                once(pe, "xp_ready", L)
                once(pe, "yacc_zero", L)
                alone(pe)
                def group(s, pb, p_count, turn):
                    def wslot(n):
                        q = MOE0 + n
                        pe.wait_ge(landed[q % RING], turn + 16 * (q // RING + 1))
                        return ring[:, q % RING, :]

                    pe.wait_ge(P_ready, p_count)
                    for k in range(K):
                        for t in range(T):
                            ins = mm(ps[:, k // 4, (k % 4) * 128:(k % 4) * 128 + 128], xp[:, t, k, :],
                                     Psel[pb][:, t, :], start=(t == 0), stop=(t == T - 1))
                    ins.then_inc(gathered, 1)
                    for t in range(T):
                        ins = pe.transpose(ps[:, 3, 256 + 128 * t:384 + 128 * t], Pw[pb][:, t, :], ident[:, :])
                    ins.then_inc(pwt_full, 1)
                    pe.wait_ge(xg_a, s + 1)
                    pe.wait_ge(xg_d, s + 1)
                    w = [wslot(n).rearrange("p (k n) -> p k n", k=K) for n in range(8)]
                    for i in range(2):
                        for k in range(K):
                            for j in range(4):
                                ins = mm(ps[32 * j:32 * j + 32, 2, i * 256:i * 256 + 256],
                                         xgT[:, k, 32 * j:32 * j + 32], w[2 * j + i][:, k, :],
                                         start=(k == 0), stop=(k == K - 1))
                    ins.then_inc(h_full, 1)
                    pe.wait_ge(h_ready, s + 1)
                    for c in range(2):
                        ins = pe.transpose(ps[:, 3, 128 * c:128 * c + 128], hperm[:, c, :], ident[:, :])
                        if c == 0:
                            ins.then_inc(ring_free, 8)
                    ins.then_inc(ht_full, 1)
                    pe.wait_ge(ht_ready, s + 1)
                    pe.wait_ge(acc_done, 2 * s + 1)
                    w = [wslot(8 + j).rearrange("p (c n) -> p c n", c=2) for j in range(4)]
                    for n in range(2):
                        for c in range(2):
                            for j in range(4):
                                ins = mm(ps[32 * j:32 * j + 32, 4 + n, :], hT[:, c, 32 * j:32 * j + 32],
                                         w[j][:, c, n * 512:n * 512 + 512], start=(c == 0), stop=(c == 1))
                    ins.then_inc(y_full, 1)
                    pe.wait_ge(y_ready, s + 1)
                    pe.wait_ge(pwt_ready, s + 1)
                    for t in range(T):
                        for n in range(2):
                            ins = mm(ps[:, (6 if t == 0 else 4) + n, :], PwT[:, 128 * t:128 * t + 128],
                                     ysb[:, n * 512:n * 512 + 512], start=True, stop=True)
                            if t == 0 and n == 0:
                                ins.then_inc(ring_free, 4)
                        ins.then_inc(c_full, 1)

                with pe.Fori(0, GROUPS // ROUND) as g:
                    for uu in range(ROUND):
                        group(L * ALLG + g * ROUND + uu, uu % 2, L * (ALLG + 1) + g * ROUND + (uu + 1),
                              L * (16 * TURNS) + g * (16 * ROUND) + 16 * uu)
                once(pe, "over_ready", L)
                alone(pe)
                n_over = pe.value_load(oe[0:1, OVER:OVER + 1], min_val=0, max_val=OVER)
                with pe.If(n_over > 0):
                    with pe.Fori(0, OVER // 4) as g:
                        group(L * ALLG + g + GROUPS, 1, L * (ALLG + 1) + g + (GROUPS + 2),
                              L * (16 * TURNS) + g * 16 + 16 * GROUPS)
                with pe.Else():
                    pe.drain()
                    for sm, n in ((gathered, 1), (pwt_full, 1), (h_full, 1), (ht_full, 1), (y_full, 1), (c_full, 2),
                                  (ring_free, 12)):
                        pe.sem_inc(sm, n * (ALLG - GROUPS))
                pe.wait_ge(acc_done, 2 * ALLG * L + 2 * ALLG + 1)

                pe_release(1)
                transposes_of_x("x2T_lo", "x2T_hi", 2, L)
                wait_xT(2, L)
                start_job("pTr", L)
                wait_unit(pe, "p", L)
                pin = unit("p")[:, 0:T * PLE].rearrange("p (t n) -> p t n", t=T)
                for i in range(2):
                    for t in range(T):
                        o = i * SEQ + t * 128
                        ins = pe.transpose(pair("pTr")[:, o:o + 128], pin[:, t, i * 128:i * 128 + 128], ident[:, :])
                end_job("pTr", ins)
                tm_pair(("pg0", "pg1"), [f"pgw{i}" for i in range(4)], xT, None)
                wait_read(pe, "pTr", L)
                pe_release(1)
                tm_pair(("pu0", "pu1"), ["pup"], pT, None)

        @block.scalar
        def _(act):
            ch = Chain(act, act_chain, ACT_CHAIN)
            link = ch.link

            def done(name, ins):
                ins.then_inc(free[job(name)[0]], 1)

            def copy_out(name, L, dst, src):
                wait_full(act, name, L)
                done(name, act.copy(dst, src))

            act.wait_ge(ev["ang_ready"], 1)
            act.activation(sin[:, :, :], sin[:, :, :], ACT.Sin)
            act.activation(cos[:, :, :], cos[:, :, :], ACT.Sin).then_inc(ev["cs_ready"], 1)

            with act.Fori(0, DEPTH) as L:
                ch.base, ch.c = L * ch.per, 0

                def xT_half(name):
                    wait_full(act, name, L)
                    done(name, act.copy(xT[:, 0:4, :].rearrange("p k n -> p (k n)"), pair(name)))

                xT_half("xT_lo")
                wait_read(act, "lat", L)
                for t in range(T):
                    act.activation(junk[:, 3 * t:3 * t + 2, :].rearrange("p a n -> p (a n)"), lat[:, t, 0:QR], ACT.Square, scale=QR ** -0.5,
                                   accum_out=st[:, 2 * t:2 * t + 1])
                    ins = act.activation(junk[:, 3 * t + 2, :], lat[:, t, QR:QR + KVR], ACT.Square, scale=KVR ** -0.5,
                                         accum_out=st[:, 2 * t + 1:2 * t + 2])
                ins.then_inc(ev["lat_squares"], 1)
                wait_full(act, "gqk", L)
                act.mul(qk[:, 0:2, :].rearrange("p a n -> p (a n)"), half("gqk", 0), DK ** -0.5)
                ins = act.copy(qk[:, 2:4, :].rearrange("p a n -> p (a n)"), half("gqk", 1))
                done("gqk", ins)
                once(act, "lat_squares", L)
                copy_out("glr", L, glrT, pair("glr")[0:LR, 0:SEQ])
                once(act, "zabs_ready", L)
                link(act.activation(za, za, ACT.Exp, scale=-1.0))
                act.activation(za, za, ACT.Ln, bias=1.0).then_inc(ev["lnz_ready"], 1)
                wait_read(act, "vecT", L)
                wait_full(act, "latT", L)
                for i in range(2):
                    act.mul(cqT[:, i, :], pair("latT")[:, i * SEQ:i * SEQ + SEQ], vecT[:, 14 + i:15 + i])
                ins = act.mul(ckvT, pair("latT")[:, 2 * SEQ:3 * SEQ], vecT[:, 16:17])
                done("latT", ins)
                copy_out("krT", L, krT.rearrange("p a n -> p (a n)"), pair("krT")[:, 0:512])
                once(act, "bcum_ready", L)
                act.activation(E1, bcum, ACT.Exp, scale=1.0 / TAU)
                act.activation(E2, bcum, ACT.Exp, scale=-1.0 / TAU)
                for i in range(2):
                    for c in range(4):
                        ins = act.activation(E3[:, i, 64 * c:64 * c + 64], bcum[:, i, 64 * c:64 * c + 64], ACT.Exp,
                                             scale=-1.0 / TAU, bias=st[:, 8 + 4 * i + c:9 + 4 * i + c])
                ins.then_inc(ev["exps_ready"], 1)
                copy_out("gv", L, vg.rearrange("p a n -> p (a n)"), pair("gv"))
                copy_out("qn", L, qnT.rearrange("p a n -> p (a n)"), pair("qn"))
                copy_out("kn", L, knT.rearrange("p a n -> p (a n)"), pair("kn"))
                copy_out("ab", L, yaT.rearrange("p a n -> p (a n)"), pair("ab"))
                copy_out("qrT", L, qrT.rearrange("p a n -> p (a n)"), pair("qrT")[:, 0:512])
                for t, sct in ((0, sc0), (1, sc1)):
                    once(act, f"max{t}_ready", L)
                    for h in range(MH):
                        ins = act.activation(sct[:, h, :], sct[:, h, :], ACT.Exp, scale=SCALE,
                                             bias=st[:, 24 + 4 * t + h:25 + 4 * t + h],
                                             accum_out=st[:, 32 + 4 * t + h:33 + 4 * t + h])
                    ins.then_inc(ev[f"exp{t}_ready"], 1)
                copy_out("ac", L, ac.rearrange("p a n -> p (a n)"), pair("ac"))
                wait_full(act, "gr", L)
                ins = act.activation(rs.rearrange("p t h n -> p (t h n)"), pair("gr"), ACT.Silu)
                done("gr", ins)
                copy_out("pT0", L, pT0.rearrange("p a n -> p (a n)"), pair("pT0"))
                copy_out("pT1", L, pT1.rearrange("p a n -> p (a n)"), pair("pT1")[:, 0:512])
                wait_full(act, "glao", L)
                for t in range(T):
                    for h in range(GH):
                        i = 40 + 4 * t + h
                        ins = act.activation(junk[:, 4 * t + h, :], half("glao", t)[:, h * 128:h * 128 + 128], ACT.Square,
                                             scale=DV ** -0.5, accum_out=st[:, i:i + 1])
                ins.then_inc(ev["o_squares"], 1)
                copy_out("yc", L, ycT.rearrange("p a n -> p (a n)"), pair("yc"))
                copy_out("ybT", L, ybT.rearrange("p a n -> p (a n)"), pair("ybT"))
                n = 0
                once(act, "ya_ready", L)
                for b in BRANCHES:
                    for h in range(2):
                        name = f"gate_{b}{h}"
                        wait_full(act, name, L)
                        if n in (2, 3):
                            wait_read(act, f"br_{BRANCHES[0]}{n - 2}", L)
                        elif n > 3:
                            act.wait_ge(sig_used, 4 * L + (n - 3))
                        done(name, act.activation(sig[n % 2].rearrange("p a n -> p (a n)"), pair(name), ACT.Sigmoid))
                        n += 1
                act.wait_ge(x_ready, 3 * L + 3)
                for t in range(T):
                    ins = act.copy(xp[:, t, :, :], x[:, t, :].rearrange("p (q k) -> p k q", k=K))
                ins.then_inc(ev["xp_ready"], 1)
                xT_half("x1T_lo")
                once(act, "gmax_ready", L)
                for t in range(T):
                    ins = act.activation(rt[:, t, 40:48], lg[:, t, 0:NG], ACT.Exp, bias=rt[:, t, 16:17],
                                         accum_out=rt[:, t, 17:18])
                ins.then_inc(ev["gexp_ready"], 1)
                once(act, "dtop_ready", L)
                act.activation(rt[:, :, 19:20], rt[:, :, 18:19], ACT.Exp).then_inc(ev["etop_ready"], 1)

                def group(s):
                    act.wait_ge(gathered, s + 1)
                    act.copy(xgT[:, 0:4, :].rearrange("p k n -> p (k n)"), ps[:, 0, :]).then_inc(xg_a, 1)
                    act.wait_ge(h_full, s + 1)
                    act.activation(silu, ps[:, 2, 0:256], ACT.Silu).then_inc(silu_ready, 1)
                    act.wait_ge(ht_full, s + 1)
                    act.copy(hT.rearrange("p c n -> p (c n)"), ps[:, 3, 0:256]).then_inc(ht_ready, 1)
                    act.wait_ge(y_full, s + 1)
                    act.copy(ysb, ps[:, 4:6, :].rearrange("p a n -> p (a n)")).then_inc(y_ready, 1)

                with act.Fori(0, GROUPS) as g:
                    group(L * ALLG + g)
                once(act, "over_ready", L)
                alone(act)
                n_over = act.value_load(oe[0:1, OVER:OVER + 1], min_val=0, max_val=OVER)
                with act.If(n_over > 0):
                    with act.Fori(0, OVER // 4) as g:
                        group(L * ALLG + g + GROUPS)
                with act.Else():
                    act.drain()
                    for sm in (xg_a, silu_ready, ht_ready, y_ready):
                        act.sem_inc(sm, ALLG - GROUPS)
                xT_half("x2T_lo")
                copy_out("pTr", L, pT.rearrange("p a n -> p (a n)"), pair("pTr")[:, 0:512])
                for n in range(2):
                    wait_read(act, f"pg{n}", L)
                    act.activation(pgs[:, n, :, :], pgs[:, n, :, :], ACT.Sigmoid).then_inc(pgs_sig, 1)
                ch.check(1)

        @block.vector
        def _(dve):
            ch = Chain(dve, dve_chain, DVE_CHAIN)
            link = ch.link

            def done(name, ins):
                ins.then_inc(free[job(name)[0]], 1)

            def signal(name, ins):
                ins.then_inc(ev[name], 1)

            def layer_norm(g_ap, b_ap, ln_wait, ready, powers):
                for t in range(T):
                    for i in range(2):
                        ins = dve.bn_stats(st6[:, t, i, :], x[:, t, 512 * i:512 * i + 512])
                link(ins)
                alone(dve)
                for t in range(T):
                    ins = dve.bn_aggr(mv[:, t, :], st6[:, t, :, :])
                ins.then_inc(power_in, 1)
                dve.wait_ge(power_out, powers)
                for t in range(T):
                    ins = dve.tensor_scalar(x[:, t, :], x[:, t, :], mv[:, t, 0:1], rstd[:, t:t + 1],
                                            ALU.subtract, ALU.mult)
                link(ins)
                ln_wait()
                for t in range(T):
                    ins = dve.tensor_tensor(x[:, t, :], x[:, t, :], g_ap, ALU.mult)
                link(ins)
                for t in range(T):
                    ins = dve.tensor_tensor(x[:, t, :], x[:, t, :], b_ap, ALU.add)
                ins.then_inc(x_ready, 1)
                dve.wait_ge(x_ready, ready)

            dve.wait_ge(pre, 48)
            layer_norm(ln0gb[:, 0, :], ln0gb[:, 1, :], lambda: None, 2, 1)
            dve.wait_ge(consts, 1)
            link(dve.tensor_copy(posf[:, :], posi[:, :]))
            for t in range(T):
                ins = dve.tensor_scalar(sin[:, t, :], inv[:, :], posf[:, t:t + 1], None, ALU.mult)
            link(ins)
            link(dve.tensor_scalar(cos[:, :, :], sin[:, :, :], float(1 / (2 * np.pi)), 12582912.0, ALU.mult, ALU.add))
            link(dve.tensor_scalar(cos[:, :, :], cos[:, :, :], 12582912.0, None, ALU.subtract))
            c1 = 6.28125
            c2 = float(np.float32(np.round((2 * np.pi - c1) * 2 ** 21) / 2 ** 21))
            c3 = float(2 * np.pi - c1 - c2)
            for c in (c1, c2, c3):
                link(dve.scalar_tensor_tensor(sin[:, :, :], cos[:, :, :], -c, sin[:, :, :], ALU.mult, ALU.add))
            pi = float(np.nextafter(np.float32(np.pi), np.float32(0)))
            link(dve.tensor_scalar(sin[:, :, :], sin[:, :, :], pi, -pi, ALU.min, ALU.max))
            link(dve.tensor_scalar(cos[:, :, :], sin[:, :, :], -1.0, None, ALU.mult))
            link(dve.tensor_tensor(cos[:, :, :], cos[:, :, :], sin[:, :, :], ALU.max))
            ins = dve.tensor_scalar(cos[:, :, :], cos[:, :, :], -1.0, float(np.pi / 2), ALU.mult, ALU.add)
            signal("ang_ready", ins)
            link(dve.memset(u[:, :, 0:2], 0.0))
            ch.check(0)
            total0 = ch.c

            with dve.Fori(0, DEPTH) as L:
                ch.base, ch.c = L * ch.per + total0, 0

                def xT_half(name):
                    wait_full(dve, name, L)
                    done(name, dve.tensor_copy(xT[:, 4:8, :].rearrange("p k n -> p (k n)"), pair(name)))

                xT_half("xT_hi")
                wait_full(dve, "vecT", L)
                ins = dve.tensor_copy(vecT[:, :], pair("vecT")[:, 0:17])
                done("vecT", ins)
                wait_read(dve, "vecT", L)
                wait_full(dve, "lat", L)
                for t in range(T):
                    ins = dve.tensor_copy(lat[:, t, :], half("lat", t)[:, 0:LAT])
                done("lat", ins)
                wait_read(dve, "lat", L)
                dve.wait_ge(ev["cs_ready"], 1)
                kx1, kx2 = lat[:, :, QR + KVR:QR + KVR + 32], lat[:, :, QR + KVR + 32:LAT]
                m = [r_[:, :, 0, :] for r_ in rope_tmp]
                dve.tensor_tensor(m[0], kx1, cos[:, :, :], ALU.mult)
                dve.tensor_tensor(m[1], kx2, sin[:, :, :], ALU.mult)
                dve.tensor_tensor(m[2], kx1, sin[:, :, :], ALU.mult)
                link(dve.tensor_tensor(m[3], kx2, cos[:, :, :], ALU.mult))
                for i in range(2):
                    dve.tensor_tensor(krp[:, :, i, 64 * i:64 * i + 32], m[0], m[1], ALU.subtract)
                    ins = dve.tensor_tensor(krp[:, :, i, 64 * i + 32:64 * i + 64], m[2], m[3], ALU.add)
                signal("kr_ready", ins)
                dve.wait_ge(power_out, 5 * L + 2)
                for t in range(T):
                    dve.tensor_scalar(lat[:, t, 0:QR], lat[:, t, 0:QR], st[:, 4 + 2 * t:5 + 2 * t], None, ALU.mult)
                    ins = dve.tensor_scalar(lat[:, t, QR:QR + KVR], lat[:, t, QR:QR + KVR],
                                            st[:, 5 + 2 * t:6 + 2 * t], None, ALU.mult)
                signal("lat_normed", ins)
                wait_full(dve, "z", L)
                for i in range(2):
                    ins = dve.tensor_scalar(zb[:, i, :], pair("z")[:, i * SEQ:i * SEQ + SEQ], vecT[:, 12 + i:13 + i],
                                            None, ALU.add)
                done("z", ins)
                wait_read(dve, "z", L)
                link(dve.tensor_scalar(za, zb, -1.0, None, ALU.mult))
                ins = dve.tensor_tensor(za, za, zb, ALU.max)
                signal("zabs_ready", ins)
                once(dve, "lnz_ready", L)
                link(dve.scalar_tensor_tensor(zb, zb, 0.0, za, ALU.min, ALU.subtract))
                for i in range(2):
                    for c in range(4):
                        o = slice(64 * c, 64 * c + 64)
                        ins = dve.tensor_tensor_scan(bcum[:, i, o], ones[:, 0:64], zb[:, i, o], 0.0, ALU.mult, ALU.add)
                link(ins)
                last = bcum.rearrange("p i (c n) -> p i c n", c=4)[:, :, :, 63]
                ins = dve.tensor_scalar(st[:, 8:16].rearrange("p (i c) -> p i c", i=2), last, 1.0 / TAU, None, ALU.mult)
                signal("bcum_ready", ins)
                once(dve, "exps_ready", L)
                wait_read(dve, "gqk", L)
                ins = dve.tensor_tensor(ktF, qk[:, 2:4, :], E3, ALU.mult)
                signal("ktF_ready", ins)
                dve.tensor_tensor(ke, qk[:, 2:4, :], E2, ALU.mult)
                for h in range(GH):
                    o = slice(64 * (h % 2), 64 * (h % 2) + 64)
                    ins = dve.tensor_tensor(qpad[o, h, :], qk[o, h // 2, :], E1[o, h // 2, :], ALU.mult)
                signal("gla_in_ready", ins)
                wait_full(dve, "qr", L)
                qv = ps[:, bank(job("qr")[0]):bank(job("qr")[0]) + 2, 0:MH * ROPE].rearrange("p t (h n) -> p t h n", h=MH)
                for t in range(T):
                    q1, q2 = qv[:, t, :, 0:32], qv[:, t, :, 32:64]
                    cb = cos[:, t, :].unsqueeze(1).to_broadcast([128, MH, 32])
                    sbb = sin[:, t, :].unsqueeze(1).to_broadcast([128, MH, 32])
                    dve.tensor_tensor(rope_tmp[0][:, t, :, :], q1, cb, ALU.mult)
                    dve.tensor_tensor(rope_tmp[1][:, t, :, :], q2, sbb, ALU.mult)
                    dve.tensor_tensor(rope_tmp[2][:, t, :, :], q1, sbb, ALU.mult)
                    ins = dve.tensor_tensor(rope_tmp[3][:, t, :, :], q2, cb, ALU.mult)
                done("qr", ins)
                wait_read(dve, "qr", L)
                dve.tensor_tensor(qr[:, :, :, 0:32], rope_tmp[0], rope_tmp[1], ALU.subtract)
                ins = dve.tensor_tensor(qr[:, :, :, 32:64], rope_tmp[2], rope_tmp[3], ALU.add)
                signal("qr_ready", ins)
                wait_full(dve, "vv", L)
                ins = dve.tensor_copy(vm.rearrange("p a n -> p (a n)"), pair("vv"))
                done("vv", ins)
                wait_full(dve, "ktT", L)
                ins = dve.tensor_copy(kt.rearrange("p t i n -> p (t i n)"), pair("ktT")[:, 0:512])
                done("ktT", ins)
                wait_full(dve, "AT", L)
                alone(dve)
                ins = dve.copy_predicated(ATm.rearrange("p t h n -> p (t h) n"),
                                          gmask[:, :].unsqueeze(1).to_broadcast([128, T * GH, 128]),
                                          pair("AT").rearrange("p (a n) -> p a n", n=128))
                done("AT", ins)

                def mask_and_max(t, name, sct, n):
                    wait_full(dve, name, L)
                    src = pair(name)[:, 0:MH * n].rearrange("p (h n) -> p h n", h=MH)
                    if t == 1:
                        dve.tensor_copy(sct[:, :, 0:128], src[:, :, 0:128])
                    ins = dve.tensor_tensor(sct[:, :, n - 128:n], src[:, :, n - 128:n],
                                            smask[:, :].unsqueeze(1).to_broadcast([128, MH, 128]), ALU.add)
                    done(name, ins)
                    wait_read(dve, name, L)
                    link(dve.tensor_reduce(st[:, 16 + 4 * t:20 + 4 * t], sct, AX.X, ALU.max))
                    ins = dve.tensor_scalar(st[:, 24 + 4 * t:28 + 4 * t], st[:, 16 + 4 * t:20 + 4 * t], -SCALE, None, ALU.mult)
                    signal(f"max{t}_ready", ins)

                def normalise(t, sct, n):
                    once(dve, f"exp{t}_ready", L)
                    link(dve.reciprocal(st[:, 48 + 4 * t:52 + 4 * t], st[:, 32 + 4 * t:36 + 4 * t]))
                    for h in range(MH):
                        ins = dve.tensor_scalar(sct[:, h, :], sct[:, h, :], st[:, 48 + 4 * t + h:49 + 4 * t + h], None, ALU.mult)
                    signal(f"soft{t}_ready", ins)

                wait_read(dve, "qrT", L)
                mask_and_max(0, "sc0", sc0, 128)
                kvp = [half("kv0", 0), half("kv0", 1), half("kv2", 0)]
                wait_full(dve, "kv0", L)
                link(dve.tensor_copy(St[:, 0, :, :].rearrange("p i n -> p (i n)"), kvp[0]))
                for c in (1, 2):
                    if c == 2:
                        wait_full(dve, "kv2", L)
                    for i in range(2):
                        ins = dve.scalar_tensor_tensor(St[:, c, i, :], St[:, c - 1, i, :],
                                                       E1[:, i, 64 * c + 63:64 * c + 64],
                                                       kvp[c][:, i * 256:i * 256 + 256], ALU.mult, ALU.add)
                    if c == 1:
                        done("kv0", ins)
                        wait_read(dve, "kv0", L)
                    else:
                        done("kv2", ins)
                normalise(0, sc0, 128)
                mask_and_max(1, "sc1", sc1, SEQ)
                normalise(1, sc1, SEQ)
                wait_read(dve, "gr", L)
                link(dve.tensor_tensor(rs.rearrange("p t h n -> p (t h) n"), rs.rearrange("p t h n -> p (t h) n"),
                                       gnorm[:, :].unsqueeze(1).to_broadcast([128, T * GH, DV]), ALU.mult))
                dve.wait_ge(power_out, 5 * L + 3)
                wait_full(dve, "glao", L)
                for t in range(T):
                    for h in range(GH):
                        ins = dve.scalar_tensor_tensor(rs[:, t, h, :], half("glao", t)[:, h * 128:h * 128 + 128],
                                                       st[:, 40 + 4 * t + h:41 + 4 * t + h], rs[:, t, h, :],
                                                       ALU.mult, ALU.mult)
                done("glao", ins)
                wait_read(dve, "ac", L)
                wait_full(dve, "ax", L)
                ins = dve.tensor_tensor(u[:, :, 2:SEQ + 2], ac, pair("ax").rearrange("p (a n) -> p a n", a=4), ALU.mult)
                done("ax", ins)
                wait_read(dve, "ax", L)
                for i in range(4):
                    ins = dve.tensor_scalar(ac[:, i, :], u[:, i, 2:SEQ + 2], vecT[:, 8 + i:9 + i], None, ALU.mult)
                link(ins)
                for tap in (1, 0):
                    for i in range(4):
                        ins = dve.scalar_tensor_tensor(ac[:, i, :], u[:, i, tap:SEQ + tap],
                                                       vecT[:, 4 * tap + i:4 * tap + i + 1], ac[:, i, :],
                                                       ALU.mult, ALU.add)
                    link(ins)
                wait_read(dve, "ab", L)
                signal("ya_ready", dve.tensor_tensor(yaT, yaT, ac, ALU.mult))
                n = 0
                for b in BRANCHES:
                    for h in range(2):
                        name = f"br_{b}{h}"
                        wait_read(dve, f"gate_{b}{h}", L)
                        wait_full(dve, name, L)
                        src = pair(name).rearrange("p (a n) -> p a n", a=4)
                        dst = merged[:, 4 * h:4 * h + 4, :]
                        if n < 2:
                            done(name, dve.tensor_tensor(dst, sig[n % 2], src, ALU.mult))
                        else:
                            ins = dve.tensor_tensor(sig[n % 2], sig[n % 2], src, ALU.mult)
                            done(name, ins)
                            wait_read(dve, name, L)
                            dve.tensor_tensor(dst, dst, sig[n % 2], ALU.add).then_inc(sig_used, 1)
                            dve.wait_ge(sig_used, 4 * L + (n - 1))
                        n += 1

                def residual(names):
                    for h, name in enumerate(names):
                        wait_full(dve, name, L)
                        for t in range(T):
                            o = slice(512 * h, 512 * h + 512)
                            ins = dve.scalar_tensor_tensor(x[:, t, o], x[:, t, o], ALPHA, half(name, t),
                                                           ALU.mult, ALU.add)
                        done(name, ins)
                    for name in names:
                        wait_read(dve, name, L)

                def ln_unit(name):
                    v = unit(name).rearrange("p (g d) -> p g d", g=2)
                    layer_norm(v[:, 0, :], v[:, 1, :], lambda: wait_unit(dve, name, L), 3 * L + 2 + int(name[2]),
                               5 * L + 3 + int(name[2]))

                residual(("wo0", "wo1"))
                ln_unit("ln1")
                xT_half("x1T_hi")
                dve.memset(yacc, 0.0).then_inc(ev["yacc_zero"], 1)
                wait_full(dve, "logit", L)
                for t in range(T):
                    ins = dve.tensor_tensor(lg[:, t, :], half("logit", t)[:, 0:NLG], br[:, :], ALU.add)
                done("logit", ins)
                wait_read(dve, "logit", L)
                alone(dve)
                for t in range(T):
                    ins = dve.max(rt[:, t, 0:8], lg[:, t, 0:NG])
                link(ins)
                for t in range(T):
                    dve.tensor_scalar(rt[:, t, 16:17], rt[:, t, 0:1], -1.0, None, ALU.mult)
                    ins = dve.max_index(idx[:, t, :], rt[:, t, 0:8], lg[:, t, 0:NG])
                signal("gmax_ready", ins)
                once(dve, "gmax_ready", L)
                link(dve.tensor_copy(rt[:, :, 20:21], idx[:, 0:2, 0:1]))
                for t in range(T):
                    ins = dve.tensor_scalar(rt[:, t, 32:40], iota[:, 0:NG], rt[:, t, 20:21], None, ALU.is_equal)
                link(ins)
                for t in range(T):
                    o = big[0].rearrange("p a b -> p (a b)")[:, 64 * t:64 * t + 64].rearrange("p (e g) -> p e g", e=EPG)
                    ins = dve.tensor_tensor(o, lg[:, t, NG:NLG].rearrange("p (g e) -> p e g", e=EPG),
                                            rt[:, t, 32:40].unsqueeze(1).to_broadcast([128, EPG, NG]), ALU.mult)
                link(ins)
                link(dve.tensor_reduce(rt[:, :, 48:56], big[0].rearrange("p a b -> p (a b)")[:, 0:128]
                                       .rearrange("p (t e g) -> p t e g", t=2, e=EPG), AX.X, ALU.add))
                alone(dve)
                for t in range(T):
                    ins = dve.max(rt[:, t, 8:16], rt[:, t, 48:56])
                link(ins)
                alone(dve)
                for t in range(T):
                    ins = dve.max_index(idx[:, 2 + t, :], rt[:, t, 8:16], rt[:, t, 48:56])
                signal("dtop_ready", dve.tensor_tensor(rt[:, :, 18:19], rt[:, :, 9:10], rt[:, :, 8:9], ALU.subtract))
                once(dve, "dtop_ready", L)
                link(dve.tensor_copy(rt[:, :, 21:23], idx[:, 2:4, 0:2]))
                for i in range(2):
                    ins = dve.scalar_tensor_tensor(rt[:, :, 25 + i:26 + i], rt[:, :, 20:21], float(EPG),
                                                   rt[:, :, 21 + i:22 + i], ALU.mult, ALU.add)
                link(ins)
                for t in range(T):
                    ins = dve.tensor_scalar(asg[:, t, :], iota[:, :], rt[:, t, 25:26], None, ALU.is_equal)
                link(ins)
                for t in range(T):
                    ins = dve.scalar_tensor_tensor(asg[:, t, :], iota[:, :], rt[:, t, 26:27], asg[:, t, :],
                                                   ALU.is_equal, ALU.add)
                signal("asg_ready", ins)
                once(dve, "etop_ready", L)
                once(dve, "gexp_ready", L)
                link(dve.scalar_tensor_tensor(rt[:, :, 23:24], rt[:, :, 19:20], 1.0, rt[:, :, 17:18], ALU.add, ALU.mult))
                link(dve.reciprocal(rt[:, :, 23:24], rt[:, :, 23:24]))
                link(dve.tensor_tensor(rt[:, :, 24:25], rt[:, :, 23:24], rt[:, :, 19:20], ALU.mult))
                for t in range(T):
                    dve.tensor_scalar(wx[:, t, 0:NE], iota[:, :], rt[:, t, 25:26], rt[:, t, 23:24], ALU.is_equal, ALU.mult)
                    ins = dve.tensor_scalar(big[0][:, t, :], iota[:, :], rt[:, t, 26:27], rt[:, t, 24:25],
                                            ALU.is_equal, ALU.mult)
                link(ins)
                link(dve.tensor_tensor(wx[:, :, 0:NE], wx[:, :, 0:NE], big[0][:, 0:2, :], ALU.add))
                wait_full(dve, "rank", L)
                rk = half("rank", 0)
                dve.scalar_tensor_tensor(rankx[:, :, 0:NE], rk[:, 0:2 * NE].rearrange("p (t e) -> p t e", t=2), 1.0,
                                         asg, ALU.add, ALU.mult)
                ins = dve.tensor_copy(cnt, rk[:, 2 * NE:3 * NE])
                done("rank", ins)
                wait_read(dve, "rank", L)
                dve.memset(rankx[:, :, NE + OVER:NR], -1.0)
                dve.memset(wx[:, :, NE + OVER:NR], 0.0)
                link(dve.tensor_scalar(rankx[:, :, 0:NE], rankx[:, :, 0:NE], 1.0, None, ALU.subtract))

                def build_P(col, pb):
                    iota_b = iota[:, 0:32].unsqueeze(1).to_broadcast([128, 4, 32])
                    for t in range(T):
                        o = Psel[pb][:, t, :].rearrange("p (j r) -> p j r", j=4)
                        ins = dve.tensor_tensor(o, rankx[:, t, col].unsqueeze(2).to_broadcast([128, 4, 32]), iota_b,
                                                ALU.is_equal)
                    link(ins)
                    for t in range(T):
                        ins = dve.tensor_tensor(Pw[pb][:, t, :].rearrange("p (j r) -> p j r", j=4),
                                                Psel[pb][:, t, :].rearrange("p (j r) -> p j r", j=4),
                                                wx[:, t, col].unsqueeze(2).to_broadcast([128, 4, 32]), ALU.mult)
                    ins.then_inc(P_ready, 1)

                build_P(slice(0, 4), 0)
                o7 = big[0].rearrange("p a b -> p (a b)")[:, 0:NE * 7].rearrange("p (e m) -> p e m", m=7)
                link(dve.tensor_tensor(o7, cnt.unsqueeze(2).to_broadcast([128, NE, 7]),
                                       iota32m[:, :].unsqueeze(1).to_broadcast([128, NE, 7]), ALU.is_gt))
                link(dve.tensor_reduce(nov, o7, AX.X, ALU.add))
                link(dve.tensor_tensor_scan(cum, ones[:, 0:NE], nov, 0.0, ALU.mult, ALU.add))
                i16 = iota[:, 0:OVER].unsqueeze(2).to_broadcast([128, OVER, NE])

                def over_e(ap):
                    return ap.unsqueeze(1).to_broadcast([128, OVER, NE])

                link(dve.tensor_tensor(big[0], over_e(cum), i16, ALU.is_le))
                dve.tensor_reduce(ov[:, 0, :], big[0], AX.X, ALU.add)
                link(dve.tensor_tensor(big[1], big[0], over_e(nov), ALU.mult))
                link(dve.tensor_reduce(ov[:, 1, :], big[1], AX.X, ALU.add))
                link(dve.tensor_tensor(ov[:, 2, :], iota[:, 0:OVER], ov[:, 1, :], ALU.subtract))
                link(dve.tensor_scalar(ov[:, 2, :], ov[:, 2, :], 1.0, 32.0, ALU.add, ALU.mult))
                dve.tensor_scalar(oe[:, 0:OVER], ov[:, 0, :], float(NE - 1), None, ALU.min)
                signal("over_ready", dve.tensor_copy(oe[:, OVER:OVER + 1], cum[:, NE - 1:NE]))
                link(dve.tensor_tensor(big[0], over_e(iota[:, :]),
                                       ov[:, 0, :].unsqueeze(2).to_broadcast([128, OVER, NE]), ALU.is_equal))
                for t in range(T):
                    dve.tensor_tensor(big[1], big[0], over_e(rankx[:, t, 0:NE]), ALU.mult)
                    link(dve.tensor_tensor(big[2], big[0], over_e(wx[:, t, 0:NE]), ALU.mult))
                    dve.tensor_reduce(rankx[:, t, NE:NE + OVER], big[1], AX.X, ALU.add)
                    link(dve.tensor_reduce(wx[:, t, NE:NE + OVER], big[2], AX.X, ALU.add))
                    link(dve.tensor_tensor(rankx[:, t, NE:NE + OVER], rankx[:, t, NE:NE + OVER], ov[:, 2, :], ALU.subtract))
                alone(dve)
                c_before = ch.c
                b_before = ch.base

                def group(s, next_P):
                    dve.wait_ge(gathered, s + 1)
                    dve.tensor_copy(xgT[:, 4:8, :].rearrange("p k n -> p (k n)"), ps[:, 1, :]).then_inc(xg_d, 1)
                    dve.wait_ge(pwt_full, s + 1)
                    dve.tensor_copy(PwT, ps[:, 3, 256:512]).then_inc(pwt_ready, 1)
                    dve.wait_ge(silu_ready, s + 1)
                    dve.tensor_tensor(hperm.rearrange("p c q -> p q c"), silu.rearrange("p (q c) -> p q c", c=2),
                                      ps[:, 2, 256:512].rearrange("p (q c) -> p q c", c=2), ALU.mult).then_inc(h_ready, 1)
                    next_P()
                    for t in range(T):
                        dve.wait_ge(c_full, 2 * s + (t + 1))
                        b = 6 if t == 0 else 4
                        dve.tensor_tensor(yacc[:, t, :], yacc[:, t, :], ps[:, b:b + 2, :].rearrange("p a n -> p (a n)"),
                                          ALU.add).then_inc(acc_done, 1)

                with dve.Fori(0, GROUPS // ROUND) as g:
                    ch.base, ch.c = b_before + g * ch.exp[2] + c_before, 0
                    for uu in range(ROUND):
                        group(L * ALLG + g * ROUND + uu,
                              lambda: build_P(bass.ds(g * (4 * ROUND) + 4 * (uu + 1), 4), (uu + 1) % 2))
                    ch.check(2)
                rounds = (GROUPS // ROUND) * ch.exp[2]
                n_over = dve.value_load(oe[0:1, OVER:OVER + 1], min_val=0, max_val=OVER)
                with dve.If(n_over > 0):
                    with dve.Fori(0, OVER // 4) as g:
                        ch.base, ch.c = b_before + g * ch.exp[3] + (c_before + rounds), 0
                        build_P(bass.ds(g * 4 + NE, 4), 1)
                        group(L * ALLG + g + GROUPS, lambda: None)
                        ch.check(3)
                with dve.Else():
                    dve.drain()
                    for sm, n in ((P_ready, 1), (xg_d, 1), (pwt_ready, 1), (h_ready, 1), (acc_done, 2),
                                  (dve_chain, ch.exp[3])):
                        dve.sem_inc(sm, n * (ALLG - GROUPS))
                ch.base, ch.c = b_before + rounds + (ALLG - GROUPS) * ch.exp[3], c_before
                dve.wait_ge(acc_done, 2 * ALLG * L + 2 * ALLG + 1)
                for t in range(T):
                    ins = dve.scalar_tensor_tensor(x[:, t, :], x[:, t, :], ALPHA, yacc[:, t, :], ALU.mult, ALU.add)
                link(ins)
                ln_unit("ln2")
                xT_half("x2T_hi")
                wait_unit(dve, "bple", L)
                for n in range(2):
                    wait_full(dve, f"pg{n}", L)
                    for t in range(T):
                        ins = dve.tensor_tensor(pgs[:, n, t, :], half(f"pg{n}", t), unit("bple")[:, 512 * n:512 * n + 512], ALU.add)
                    done(f"pg{n}", ins)
                for n in range(2):
                    dve.wait_ge(pgs_sig, 2 * L + (n + 1))
                    wait_full(dve, f"pu{n}", L)
                    for t in range(T):
                        ins = dve.tensor_tensor(pgs[:, n, t, :], pgs[:, n, t, :], half(f"pu{n}", t), ALU.mult)
                    done(f"pu{n}", ins)
                    wait_read(dve, f"pu{n}", L)
                    for t in range(T):
                        o = slice(512 * n, 512 * n + 512)
                        ins = dve.scalar_tensor_tensor(x[:, t, o], x[:, t, o], ALPHA, pgs[:, n, t, :], ALU.mult, ALU.add)
                link(ins)
                ln_unit("ln3")
                ch.check(1)


def kernel(**inputs):
    import concourse.bacc as bacc
    from concourse.bass_utils import run_bass_kernel_spmd

    arr = {k: np.ascontiguousarray(v) for k, v in inputs.items()}
    lay = {
        "x": arr["x"], "positions": arr["positions"],
        "p": arr["p"].reshape(DEPTH, SEQ, PLE),
        "ln0": np.stack([arr["ln0_g"], arr["ln0_b"]]),
        "w_exp": arr["w_exp"].reshape(DEPTH, D, NE), "b_exp": arr["b_exp"].reshape(DEPTH, NE),
        "w_gate": arr["w_gate"].reshape(DEPTH * NE, D, HID), "w_up": arr["w_up"].reshape(DEPTH * NE, D, HID),
        "w_down": arr["w_down"].reshape(DEPTH * NE, HID, D),
    }
    for i in (1, 2, 3):
        lay[f"ln{i}"] = np.stack([arr[f"ln{i}_g"], arr[f"ln{i}_b"]], axis=1)
    for n in ("w_in", "w_conv", "w_gla_gate", "b_gla_gate", "gla_norm_g", "mla_q_norm_g", "mla_kv_norm_g", "w_uq",
              "w_ukv", "w_br", "w_o", "w_grp", "b_grp", "w_ple_gate", "b_ple_gate", "w_ple_up"):
        lay[n] = arr[n]
    nc = bacc.Bacc("TRN2", target_bir_lowering=False, num_devices=1)
    aps = {n: nc.dram_tensor(f"in_{n}", v.shape, mybir.dt.from_np(v.dtype), kind="ExternalInput").ap()
           for n, v in lay.items()}
    aps["out"] = nc.dram_tensor("out", (1, SEQ, D), F32, kind="ExternalOutput").ap()
    build(nc, aps)
    r = run_bass_kernel_spmd(nc, [{f"in_{n}": v for n, v in lay.items()}], core_ids=[0])
    return r.results[0]["out"]
```

```python
from contextlib import ExitStack

import numpy as np

import concourse.bass as bass
from concourse import mybir

F32 = mybir.dt.float32
I32 = mybir.dt.int32
U32 = mybir.dt.uint32
ALU = mybir.AluOpType
ACT = mybir.ActivationFunctionType
AX = mybir.AxisListType

D, SEQ, DEPTH, PLE = 1024, 256, 2, 256
T, K = SEQ // 128, D // 128
SC, GH, DK, DV, LR, CH = 512, 4, 64, 128, 16, 64
TAU = 16.0
MH, NOPE, ROPE, MV, QR, KVR = 4, 128, 64, 128, 256, 128
NG, EPG, NE, HID = 8, 8, 64, 256
ALPHA = float((2 * DEPTH) ** 0.25)
LN_EPS, RMS_EPS = 1e-5, 1e-6
SCALE = float((NOPE + ROPE) ** -0.5)
NLG = NG + NE

C_B, C_C, C_X = 0, SC, 2 * SC
C_QK = 3 * SC
C_V = C_QK + 2 * GH * DK
C_LR = C_V + GH * DV
C_R = C_LR + LR
C_LAT = C_R + GH * DV
LAT = QR + KVR + ROPE
C_GATE = C_LAT + LAT

RING = 12
SLOT = 2048
GROUPS = NE // 4
OVER = 16
ALLG = GROUPS + OVER // 4
ROUND = 4

JOBS = ["xT_lo", "xT_hi", "lat", "gqk", "vecT", "glr", "z", "latT", "krT", "gv", "qn", "qr", "kn", "vv",
        "ktT", "ab", "qrT", "AT", "sc0", "kv0", "kv2", "sc1", "ac", "gr", "pT0", "pT1", "glao", "ax",
        "yc", "ybT"]
BRANCHES = ("a", "c", "b")
BROW = {"a": 0, "b": 1, "c": 2}
for _b in BRANCHES:
    for _h in range(2):
        JOBS += [f"gate_{_b}{_h}", f"br_{_b}{_h}"]
JOBS += ["wo0", "wo1", "pTr", "pu0", "x1T_lo", "x1T_hi", "logit", "pu1", "rank", "x2T_lo", "x2T_hi", "pg0", "pg1"]
JOBS_OF = [len(JOBS[p::4]) for p in range(4)]

UNITS = ["lat0", "lat1", "gqk0", "gqk1", "gv0", "gv1", "uq", "ukv", "ab0", "ab1", "ac0", "ac1", "gr0", "gr1",
         "ax0", "ax1"]
for _b in BRANCHES:
    for _h in range(2):
        UNITS += [f"gate_{_b}{_h}0", f"gate_{_b}{_h}1", f"wbr_{_b}{_h}"]
UNITS += ["wo_0", "wo_1", "wo_2", "wo_3", "p", "pup", "ln1"]
MOE0 = len(UNITS)
MOE_UNITS = ALLG * 12
TAIL = ["pgw0", "pgw1", "pgw2", "pgw3", "bple", "ln2", "ln3"]
TAIL0 = MOE0 + MOE_UNITS
PER_LAYER = TAIL0 + len(TAIL)
assert PER_LAYER % RING == 0, PER_LAYER
TURNS = PER_LAYER // RING
SMALL_LOADS = 14
CARRIED = 3

IDLE = {"third LayerNorm": 10, "xT": 2, "x1T": 2, "router": 4, "first P": 2, "hidden": 4,
        "second LayerNorm": 10, "x2T": 2}

DVE_CHAIN = (13, 46, 4, 1, 13)
ACT_CHAIN = (0, 1, 0, 0, 0)



def build(nc, a):
    ctx = ExitStack()
    with ctx:
        def sb(name, shape, dt=F32):
            return ctx.enter_context(nc.sbuf_tensor(name, shape, dt))

        def sem(name):
            return ctx.enter_context(nc.semaphore(name))

        ring = sb("ring", [128, RING, SLOT])
        x = sb("x", [128, T, D])
        xT = sb("xT", [128, K, SEQ])
        ident = sb("ident", [128, 128])
        gmask = sb("gmask", [128, 128], I32)
        smask = sb("smask", [128, 128])
        tri = sb("tri", [128, 128])
        ones = sb("ones", [128, 128])
        iota = sb("iota", [128, NE])
        iota32m = sb("iota32m", [128, 7])
        cos = sb("cos", [128, T, ROPE // 2])
        sin = sb("sin", [128, T, ROPE // 2])
        qpad = sb("qpad", [128, GH, SEQ])
        ATm = sb("ATm", [128, T, GH, 128])
        krp = sb("krp", [128, T, 2, 128])
        wlr = sb("wlr", [128, K, LR])
        wgg = sb("wgg", [LR, GH * DK])
        gnorm = sb("gnorm", [128, DV])
        vec = sb("vec", [65, 128])
        vecT = sb("vecT", [128, 65])
        lnT = sb("lnT", [128, 16])
        wr = sb("wr", [128, K, NLG])
        br = sb("br", [128, NLG])
        st = sb("st", [128, 64])
        minus_half = sb("minus_half", [128, 8])
        st6 = sb("st6", [128, T, 2, 6])
        mv = sb("mv", [128, T, 2])
        rstd = sb("rstd", [128, T])

        NS = 19592
        S = sb("scratch", [128, NS])
        used = [0]

        def area(n):
            o = used[0]
            used[0] += n
            assert used[0] <= NS, used[0]
            return o

        def v2(o, *dims):
            n = int(np.prod(dims))
            ap = S[:, o:o + n]
            if len(dims) == 1:
                return ap
            if len(dims) == 2:
                return ap.rearrange("p (a b) -> p a b", a=dims[0])
            if len(dims) == 3:
                return ap.rearrange("p (a b c) -> p a b c", a=dims[0], b=dims[1])

        oM = area(4096)
        merged = v2(oM, K, SEQ)
        sig = [v2(oM + 2048, 4, SEQ), v2(oM + 3072, 4, SEQ)]
        qk = v2(oM, 4, SEQ)
        zb = v2(oM + 1024, 2, SEQ)
        za = v2(oM + 1536, 2, SEQ)
        bcum = v2(oM + 2048, 2, SEQ)
        E3 = v2(oM + 2560, 2, SEQ)
        ktF = v2(oM + 3072, 2, SEQ)
        ke = v2(oM + 3584, 2, SEQ)
        oE = area(1024)
        E1 = v2(oE, 2, SEQ)
        E2 = v2(oE + 512, 2, SEQ)
        kt = v2(area(512), T, 2, 128)
        vg = v2(area(1024), T, 512)
        rs = v2(area(1024), T, GH, DV)
        St = v2(area(1536), 3, 2, 256)
        oL = area(896 + 512 + 256)
        lat = v2(oL, T, LAT)
        cqT = v2(oL + 896, 2, SEQ)
        ckvT = v2(oL + 896 + 512, SEQ)
        pT0 = v2(oL, MH, SEQ)
        pT1 = v2(oL + 1024, MH, 128)
        krT = v2(area(512), 2, SEQ)
        oQ = area(1024)
        qnT = v2(oQ, MH, SEQ)
        ycT = v2(oQ, MH, SEQ)
        qrT = v2(area(512), 2, SEQ)
        oK = area(1024)
        knT = v2(oK, MH, SEQ)
        ybT = v2(oK, GH, SEQ)
        vm = v2(area(1024), T, 512)
        oS = area(1536)
        sc0 = v2(oS, MH, 128)
        sc1 = v2(oS + 512, MH, SEQ)
        qr = v2(oS, T, MH, ROPE)
        rope_tmp = [v2(oS + 512 + 256 * i, T, MH, ROPE // 2) for i in range(4)]
        yaT = v2(area(1024), 4, SEQ)
        ac = v2(area(1024), 4, SEQ)
        u = v2(area(4 * (SEQ + 2)), 4, SEQ + 2)
        inv = v2(oK + 128, ROPE // 2)
        posf = v2(oK + 512, T)
        posi = v2(oK + 520, T).bitcast(I32)
        ln0rows = S[0:16, oK:oK + 128]
        yT = {"a": yaT, "b": ybT, "c": ycT}
        junk = v2(oE, 8, 128)
        glrT = za[0:LR, 0, :]
        gmask_f = qk[:, 0, 0:128]
        used[0] = 0
        xp = v2(area(2048), T, K, 128)
        yacc = v2(area(2048), T, D)
        Psel = [v2(area(256), T, 128) for _ in range(2)]
        Pw = [v2(area(256), T, 128) for _ in range(2)]
        xgT = v2(area(1024), K, 128)
        silu = v2(area(256), 256)
        hperm = v2(area(256), 2, 128)
        hT = v2(area(256), 2, 128)
        PwT = v2(area(256), 256)
        ysb = v2(area(1024), D)
        NR = 4 * (ALLG + 1)
        rankx = v2(area(T * NR), T, NR)
        wx = v2(area(T * NR), T, NR)
        asg = v2(area(T * NE), T, NE)
        lg = v2(area(T * NLG), T, NLG)
        rt = v2(area(T * 64), T, 64)
        nov = v2(area(NE), NE)
        cum = v2(area(NE), NE)
        big = [v2(area(OVER * NE), OVER, NE) for _ in range(3)]
        ov = v2(area(4 * OVER), 4, OVER)
        cnt = v2(area(NE), NE)
        oe = sb("oe", [128, OVER + 1], I32)
        idx = sb("idx", [128, 4, 8], U32)
        pgs = v2(4096, 2, T, 512)
        used[0] = max(used[0], 12288)
        pT = v2(area(512), 2, SEQ)
        pus = v2(area(2048), 2, T, 512)

        ps = ctx.enter_context(nc.psum_tensor("ps", [128, 8, 512], F32))

        full = [sem(f"job_full{p}") for p in range(4)]
        free = [sem(f"job_free{p}") for p in range(4)]
        landed = [sem(f"landed{i}") for i in range(RING)]
        ring_free = sem("ring_free")
        x_ready = sem("x_ready")
        small = sem("small_loads")
        pre, pre_vec = sem("first_loads"), sem("first_vec")
        ln0_full, lnT_ready, xfinal = sem("ln0_full"), sem("lnT_ready"), sem("x_final")
        inv_ready = sem("inv_ready")
        consts, ident_ready = sem("consts"), sem("ident_ready")
        dve_chain, act_chain = sem("dve_chain"), sem("act_chain")
        pool_chain = sem("pool_chain")
        ev = {n: sem(n) for n in (
            "lat_squares lat_normed kr_ready zabs_ready lnz_ready "
            "bcum_ready exps_ready gla_in_ready ktF_ready qr_ready "
            "ya_ready max0_ready exp0_ready "
            "soft0_ready max1_ready exp1_ready soft1_ready o_squares "
            "xp_ready gmax_ready gexp_ready dtop_ready etop_ready asg_ready over_ready table_ready "
            "yacc_zero cs_ready ang_ready").split()}
        sig_used, pgs_sig = sem("sig_used"), sem("ple_sigmoid")
        P_ready, gathered, xg_a, xg_d = sem("P_ready"), sem("gathered"), sem("xg_by_act"), sem("xg_by_dve")
        pwt_full, pwt_ready = sem("pwt_full"), sem("pwt_ready")
        h_full, silu_ready, h_ready = sem("h_full"), sem("silu_ready"), sem("h_ready")
        ht_full, ht_ready = sem("ht_full"), sem("ht_ready")
        y_full, y_ready = sem("y_full"), sem("y_ready")
        c_full, acc_done = sem("c_full"), sem("acc_done")
        out_done = sem("out_done")
        passed = sem("waits_passed")
        power_in, power_out = sem("power_in"), sem("power_out")
        eps_added = sem("eps_added")

        def bank(p, i=0):
            return 2 * (p % 4) + i

        def job(name):
            n = JOBS.index(name)
            return n % 4, n // 4

        def pair(name):
            p = job(name)[0]
            return ps[:, 2 * p:2 * p + 2, :].rearrange("p a b -> p (a b)")

        def half(name, i):
            return ps[:, 2 * job(name)[0] + i, :]

        def wait_full(eng, name, L):
            p, i = job(name)
            eng.wait_ge(full[p], L * JOBS_OF[p] + (i + 1))

        def wait_free(eng, name, L):
            p, i = job(name)
            eng.wait_ge(free[p], L * JOBS_OF[p] + (i + 1))

        def wait_read(eng, name, L):
            p, i = job(name)
            eng.wait_ge(free[p], L * JOBS_OF[p] + (i + 2))
            alone(eng)

        def unit_pos(name):
            return UNITS.index(name) if name in UNITS else TAIL0 + TAIL.index(name)

        def unit(name):
            return ring[:, unit_pos(name) % RING, :]

        def early(q):
            return 16 if q % RING == (PER_LAYER - 1) % RING else 0

        def wait_unit(eng, name, L):
            q = unit_pos(name)
            eng.wait_ge(landed[q % RING], L * (16 * TURNS) + (16 * (q // RING + 1) + early(q)))

        def once(eng, name, L):
            eng.wait_ge(ev[name], L + 1)

        def alone(eng):
            eng.sem_inc(passed, 1)

        class Chain:

            def __init__(self, eng, s, expected):
                self.eng, self.s, self.exp = eng, s, expected
                self.base, self.c = 0, 0
                self.per = expected[1] + (GROUPS // ROUND) * expected[2] + (ALLG - GROUPS) * expected[3] + expected[4]

            def link(self, ins):
                self.c += 1
                ins.then_inc(self.s, 1)
                self.eng.wait_ge(self.s, self.base + self.c)

            def check(self, i):
                assert self.c == self.exp[i], (self.s, i, self.c)

        block = ctx.enter_context(nc.Block())

        @block.sync
        def _(sp):
            def issue(q, L, src, dst):
                sp.wait_ge(ring_free, L * PER_LAYER + (q + 1))
                alone(sp)
                sp.dma_start(dst, src).then_inc(landed[q % RING], 16)

            def w_rows(w, L, r0, nk, c0, nc_):
                return w[bass.ds(L, 1), r0:r0 + 128 * nk, c0:c0 + nc_].rearrange("l (k p) n -> p (l k) n", p=128)

            def rows_unit(q, L, w, r0, nk, c0, nc_):
                dst = ring[:, q % RING, 0:nk * nc_].rearrange("p (k n) -> p k n", k=nk)
                issue(q, L, w_rows(w, L, r0, nk, c0, nc_), dst)

            def small_loads(L):
                sp.wait_ge(x_ready, 3 * L + 1)
                alone(sp)
                sp.dma_start(wlr[:, :, :], a["w_in"][bass.ds(L, 1), :, C_LR:C_LR + LR]
                               .rearrange("l (k p) n -> p (l k) n", p=128)).then_inc(small, 16)
                sp.dma_start(wgg[:, :], a["w_gla_gate"][bass.ds(L, 1), :, :].rearrange("l r n -> (l r) n")).then_inc(small, 16)
                sp.dma_start(gnorm[:, :], a["gla_norm_g"][bass.ds(L, 1), :].to_broadcast([128, DV])).then_inc(small, 16)
                sp.dma_start(vec[0:12, :], a["w_conv"][bass.ds(L, 1), :, :].rearrange("l k (t p) -> (l k t) p", p=128)).then_inc(small, 16)
                sp.dma_start(vec[12:14, :], a["b_gla_gate"][bass.ds(L, 1), :].rearrange("l (t p) -> (l t) p", p=128)).then_inc(small, 16)
                sp.dma_start(vec[14:16, :], a["mla_q_norm_g"][bass.ds(L, 1), :].rearrange("l (t p) -> (l t) p", p=128)).then_inc(small, 16)
                sp.dma_start(vec[16:17, :], a["mla_kv_norm_g"][bass.ds(L, 1), :]).then_inc(small, 16)
                sp.dma_start(wr[:, :, 0:NG], a["w_grp"][bass.ds(L, 1), :, :].rearrange("l (k p) n -> p (l k) n", p=128)).then_inc(small, 16)
                sp.dma_start(wr[:, :, NG:NLG], a["w_exp"][bass.ds(L, 1), :, :].rearrange("l (k p) n -> p (l k) n", p=128)).then_inc(small, 16)
                sp.dma_start(br[:, 0:NG], a["b_grp"][bass.ds(L, 1), :].to_broadcast([128, NG])).then_inc(small, 16)
                sp.dma_start(br[:, NG:NLG], a["b_exp"][bass.ds(L, 1), :].to_broadcast([128, NE])).then_inc(small, 16)
                for i in range(3):
                    sp.dma_start(vec[17 + 16 * i:33 + 16 * i, :], a[f"ln{i + 1}"][bass.ds(L, 1), :, :]
                                 .rearrange("l g (k p) -> (l g k) p", p=128)).then_inc(small, 16)

            starts = {"gqk": C_QK, "gv": C_V, "ab": C_B, "ac": C_C, "ax": C_X, "gr": C_R}
            with sp.Fori(0, DEPTH) as L:
                for q, name in enumerate(UNITS):
                    if q == 4:
                        small_loads(L)
                    if name in ("lat0", "lat1"):
                        rows_unit(q, L, a["w_in"], 512 * int(name[-1]), 4, C_LAT, LAT)
                    elif name[:-1] in starts:
                        rows_unit(q, L, a["w_in"], 512 * int(name[-1]), 4, starts[name[:-1]], 512)
                    elif name == "uq":
                        rows_unit(q, L, a["w_uq"], 0, 2, 0, MH * (NOPE + ROPE))
                    elif name == "ukv":
                        rows_unit(q, L, a["w_ukv"], 0, 1, 0, MH * (NOPE + MV))
                    elif name.startswith("gate_"):
                        c0 = C_GATE + D * BROW[name[5]] + 512 * int(name[6])
                        rows_unit(q, L, a["w_in"], 512 * int(name[7]), 4, c0, 512)
                    elif name.startswith("wbr_"):
                        rows_unit(q, L, a["w_br"], 512 * BROW[name[4]], 4, 512 * int(name[5]), 512)
                    elif name.startswith("wo_"):
                        rows_unit(q, L, a["w_o"], 256 * int(name[3]), 2, 0, D)
                    elif name == "ln1":
                        issue(q, L, a["ln1"][bass.ds(L, 1), :, :].rearrange("l g d -> l (g d)")
                              .to_broadcast([128, 2 * D]), ring[:, q % RING, :])
                    elif name == "p":
                        rows_unit(q, L, a["p"], 0, T, 0, PLE)
                    elif name == "pup":
                        rows_unit(q, L, a["w_ple_up"], 0, 2, 0, D)

                def load_group(base, experts):
                    n = 0
                    for w in (a["w_gate"], a["w_up"]):
                        for j in range(4):
                            q = MOE0 + n
                            sp.wait_ge(ring_free, base + (MOE0 + n + 1))
                            alone(sp)
                            sp.dma_start(ring[:, q % RING, :],
                                         w[bass.ds(experts[j], 1), :, :].rearrange("e (p k) n -> p (e k n)", k=K)
                                         ).then_inc(landed[q % RING], 16)
                            n += 1
                    for j in range(4):
                        q = MOE0 + n
                        sp.wait_ge(ring_free, base + (MOE0 + n + 1))
                        alone(sp)
                        sp.dma_start(ring[:, q % RING, :],
                                     a["w_down"][bass.ds(experts[j], 1), :, :].rearrange("e (p c) n -> p (e c n)", c=2)
                                     ).then_inc(landed[q % RING], 16)
                        n += 1

                with sp.Fori(0, GROUPS) as s:
                    load_group(L * PER_LAYER + s * 12, [L * NE + s * 4 + j for j in range(4)])
                once(sp, "over_ready", L)
                alone(sp)
                n_over = sp.value_load(oe[0:1, OVER:OVER + 1], min_val=0, max_val=OVER)
                with sp.If(n_over > 0):
                    once(sp, "table_ready", L)
                    alone(sp)
                    with sp.Fori(0, OVER // 4) as g:
                        es = [sp.value_load(oe[0:1, bass.ds(g * 4 + j, 1)], min_val=0, max_val=NE - 1)
                              for j in range(4)]
                        load_group(L * PER_LAYER + g * 12 + GROUPS * 12, [L * NE + e for e in es])
                with sp.Else():
                    for i in range(RING):
                        q = MOE0 + 12 * (GROUPS - 1) + i
                        sp.wait_ge(landed[q % RING], L * (16 * TURNS) + (16 * (q // RING + 1) + early(q)))
                        alone(sp)
                    for i in range(RING):
                        sp.sem_inc(landed[i], 16 * (ALLG - GROUPS))
                for i, name in enumerate(TAIL):
                    q = TAIL0 + i
                    if name in ("ln2", "ln3"):
                        issue(q, L, a[name][bass.ds(L, 1), :, :].rearrange("l g d -> l (g d)")
                              .to_broadcast([128, 2 * D]), ring[:, q % RING, :])
                    elif name.startswith("pgw"):
                        rows_unit(q, L, a["w_ple_gate"], 256 * int(name[3]), 2, 0, D)
                    elif name == "bple":
                        issue(q, L, a["b_ple_gate"][bass.ds(L, 1), :].to_broadcast([128, D]), ring[:, q % RING, 0:D])
            for t in range(T):
                sp.wait_ge(xfinal, 3 * DEPTH + 1)
                sp.dma_start(a["out"][0, 128 * t:128 * t + 128, :], x[:, t, :]).then_inc(out_done, 16)
            sp.wait_ge(out_done, 16 * T)

        @block.gpsimd
        def _(pool):
            pool.memset(st[:, 62:63], 0.0).then_inc(ring_free, RING - CARRIED)
            for sm in (*free, x_ready, acc_done):
                pool.sem_inc(sm, 1)
            n = 1

            def c(ins):
                nonlocal n
                n += 1
                ins.then_inc(pool_chain, 1)
                pool.wait_ge(pool_chain, n)

            pool.memset(ident[:, :], 0.0).then_inc(pool_chain, 1)
            pool.wait_ge(pool_chain, 1)
            pool.affine_select(out=ident[:, :], in_=ident[:, :], compare_op=ALU.not_equal, fill=1.0, base=0,
                               pattern=[[-1, 128]], channel_multiplier=1).then_inc(ident_ready, 1)
            for i in range(ROPE // 2):
                ins = pool.memset(inv[:, i:i + 1], float(np.float32(1.0) / np.float32(10000.0) ** (np.float32(2 * i) / np.float32(ROPE))))
            ins.then_inc(inv_ready, 1)
            pool.memset(gmask_f[:, :], 1.0)
            pool.memset(smask[:, :], 0.0)
            pool.memset(ones[:, :], 1.0)
            pool.memset(tri[:, :], 1.0)
            pool.memset(qpad[:, :, :], 0.0)
            pool.memset(minus_half[:, :], -0.5)
            pool.memset(ATm[:, :, :, :], 0.0)
            c(pool.memset(krp[:, :, :, :], 0.0))
            pool.affine_select(out=gmask_f[:, :], in_=gmask_f[:, :], compare_op=ALU.is_ge, fill=0.0, base=0,
                               pattern=[[1, 128]], channel_multiplier=-1)
            pool.affine_select(out=smask[:, :], in_=smask[:, :], compare_op=ALU.is_ge, fill=-1e30, base=0,
                               pattern=[[-1, 128]], channel_multiplier=1)
            pool.affine_select(out=tri[:, :], in_=tri[:, :], compare_op=ALU.is_gt, fill=0.0, base=0,
                               pattern=[[1, 128]], channel_multiplier=-1)
            pool.iota(iota[:, :], [[1, NE]], base=0, channel_multiplier=0, allow_small_or_imprecise_dtypes=True)
            c(pool.iota(iota32m[:, :], [[32, 7]], base=32, channel_multiplier=0, allow_small_or_imprecise_dtypes=True))
            c(pool.memset(gmask_f[0:64, 64:128], 0.0))
            c(pool.tensor_copy(gmask[:, :], gmask_f[:, :]))
            pool.memset(st[:, 63:64], 0.0).then_inc(consts, 1)
            def rsqrt(out, ms, eps, n):
                pool.tensor_scalar(out, ms, eps, None, ALU.add).then_inc(eps_added, 1)
                pool.wait_ge(eps_added, n)
                pool.tensor_tensor(out, out, minus_half[:, 0:out.shape[1]], ALU.pow).then_inc(power_out, 1)

            pool.wait_ge(power_in, 1)
            rsqrt(rstd[:, :], mv[:, :, 1], LN_EPS, 1)
            with pool.Fori(0, DEPTH) as L:
                once(pool, "lat_squares", L)
                alone(pool)
                rsqrt(st[:, 4:8], st[:, 0:4], RMS_EPS, 5 * L + 2)
                once(pool, "o_squares", L)
                alone(pool)
                rsqrt(st[:, 40:48], st[:, 40:48], RMS_EPS, 5 * L + 3)
                for i in range(3):
                    pool.wait_ge(power_in, 3 * L + (i + 2))
                    alone(pool)
                    rsqrt(rstd[:, :], mv[:, :, 1], LN_EPS, 5 * L + (i + 4))
                    if i == 0:
                        pool.memset(yacc, 0.0).then_inc(ev["yacc_zero"], 1)

        @block.tensor
        def _(pe):
            mm = pe.matmul

            def start_job(name, L):
                wait_free(pe, name, L)

            def end_job(name, ins):
                ins.then_inc(full[job(name)[0]], 1)

            def fm(name, units, L, nk=K, rhs=None, m_of=None):
                for un in units:
                    wait_unit(pe, un, L)
                start_job(name, L)
                per = nk // len(units)
                w = [unit(un).rearrange("p (k n) -> p k n", k=per) for un in units]
                out = pair(name)
                for m in range(4):
                    for k in range(nk):
                        ins = mm(out[:, m * SEQ:m * SEQ + SEQ], w[k // per][:, k % per, m * 128:m * 128 + 128],
                                 rhs[:, k, :], start=(k == 0), stop=(k == nk - 1))
                        if m == 0 and k == 0:
                            flush(ins)
                end_job(name, ins)
                pe_release(len(units))

            def tm(name, units, L, ncols):
                for un in units:
                    wait_unit(pe, un, L)
                start_job(name, L)
                w = [unit(un)[:, 0:4 * ncols].rearrange("p (k n) -> p k n", k=4) for un in units]
                for t in range(T):
                    for k in range(K):
                        ins = mm(half(name, t)[:, 0:ncols], xT[:, k, 128 * t:128 * t + 128], w[k // 4][:, k % 4, :],
                                 start=(k == 0), stop=(k == K - 1))
                        if t == 0 and k == 0:
                            flush(ins)
                end_job(name, ins)
                pe_release(len(units))

            pending = [0]

            def pe_release(n):
                pending[0] += n

            def flush(ins):
                if pending[0]:
                    ins.then_inc(ring_free, pending[0])
                    pending[0] = 0

            def keep_clock(out, n):
                for _ in range(n):
                    mm(out, ident[:, :], ident[:, :].unsqueeze(1).to_broadcast([128, 4, 128]), start=True, stop=True)

            def transposes_of_x(lo, hi, rnd, L, idle=0):
                start_job(lo, L)
                keep_clock(half(lo, 0).rearrange("p (a n) -> p a n", a=4), idle)
                pe.wait_ge(x_ready, 3 * L + (rnd + 2))
                for n, name in enumerate((lo, hi)):
                    if n == 1:
                        start_job(name, L)
                    for kk in range(4):
                        k = 4 * n + kk
                        for t in range(T):
                            o = kk * SEQ + t * 128
                            ins = pe.transpose(pair(name)[:, o:o + 128], x[:, t, k * 128:k * 128 + 128], ident[:, :])
                            if kk == 0 and t == 0:
                                flush(ins)
                    end_job(name, ins)

            def wait_xT(rnd, L, first, idle):
                start_job(first, L)
                keep_clock(half(first, 0).rearrange("p (a n) -> p a n", a=4), idle)
                for part in ("lo", "hi"):
                    wait_read(pe, ("xT_", "x1T_", "x2T_")[rnd] + part, L)

            pe.wait_ge(ident_ready, 1)
            pe.wait_ge(pre_vec, 16)
            pe.transpose(ps[:, 6, 0:16], ln0rows, ident[0:16, 0:16]).then_inc(ln0_full, 1)
            with pe.Fori(0, DEPTH) as L:
                pending[0] = 2
                transposes_of_x("xT_lo", "xT_hi", 0, L, idle=IDLE["third LayerNorm"])
                wait_xT(0, L, "lat", IDLE["xT"])
                tm("lat", ("lat0", "lat1"), L, LAT)
                pe.wait_ge(xfinal, 3 * L + 1)
                pe_release(1)
                fm("gqk", ("gqk0", "gqk1"), L, rhs=xT)

                pe.wait_ge(small, L * (16 * SMALL_LOADS) + 16 * SMALL_LOADS)
                start_job("vecT", L)
                alone(pe)
                end_job("vecT", pe.transpose(pair("vecT")[:, 0:65], vec[:, :], ident[0:65, 0:65]))
                start_job("glr", L)
                for k in range(K):
                    ins = mm(pair("glr")[0:LR, 0:SEQ], wlr[:, k, :], xT[:, k, :], start=(k == 0), stop=(k == K - 1))
                    if k == 0:
                        flush(ins)
                end_job("glr", ins)

                wait_read(pe, "glr", L)
                start_job("z", L)
                for i in range(2):
                    ins = mm(pair("z")[:, i * SEQ:i * SEQ + SEQ], wgg[:, i * 128:i * 128 + 128], glrT,
                             start=True, stop=True)
                end_job("z", ins)

                pe.wait_ge(consts, 1)
                once(pe, "lat_normed", L)
                start_job("latT", L)
                for i in range(3):
                    for t in range(T):
                        o = i * SEQ + t * 128
                        ins = pe.transpose(pair("latT")[:, o:o + 128], lat[:, t, i * 128:i * 128 + 128], ident[:, :])
                end_job("latT", ins)
                once(pe, "kr_ready", L)
                start_job("krT", L)
                for i in range(2):
                    for t in range(T):
                        o = i * SEQ + t * 128
                        ins = pe.transpose(pair("krT")[:, o:o + 128], krp[:, t, i, :], ident[:, :])
                end_job("krT", ins)

                tm("gv", ("gv0", "gv1"), L, 512)

                wait_read(pe, "latT", L)
                wait_unit(pe, "uq", L)
                start_job("qn", L)
                wuq = unit("uq")[:, 0:2 * MH * (NOPE + ROPE)].rearrange("p (k h n) -> p k h n", k=2, h=MH)
                first = True
                for h in range(MH):
                    for k in range(2):
                        ins = mm(pair("qn")[:, h * SEQ:h * SEQ + SEQ], wuq[:, k, h, 0:NOPE], cqT[:, k, :],
                                 start=(k == 0), stop=(k == 1))
                        if first:
                            flush(ins)
                            first = False
                end_job("qn", ins)
                start_job("qr", L)
                for t in range(T):
                    for k in range(2):
                        ins = mm(half("qr", t)[:, 0:MH * ROPE], cqT[:, k, 128 * t:128 * t + 128],
                                 wuq[:, k, :, NOPE:NOPE + ROPE], start=(k == 0), stop=(k == 1))
                end_job("qr", ins)
                wait_unit(pe, "ukv", L)
                wukv = unit("ukv")[:, 0:MH * (NOPE + MV)].rearrange("p (h n) -> p h n", h=MH)
                start_job("kn", L)
                for h in range(MH):
                    ins = mm(pair("kn")[:, h * SEQ:h * SEQ + SEQ], wukv[:, h, 0:NOPE], ckvT, start=True, stop=True)
                end_job("kn", ins)
                start_job("vv", L)
                for t in range(T):
                    ins = mm(half("vv", t), ckvT[:, 128 * t:128 * t + 128], wukv[:, :, NOPE:NOPE + MV],
                             start=True, stop=True)
                end_job("vv", ins)
                pe_release(2)

                once(pe, "ktF_ready", L)
                start_job("ktT", L)
                for t in range(T):
                    for i in range(2):
                        o = (t * 2 + i) * 128
                        ins = pe.transpose(pair("ktT")[:, o:o + 128], ktF[:, i, 128 * t:128 * t + 128], ident[:, :])
                        if t == 0 and i == 0:
                            flush(ins)
                end_job("ktT", ins)

                fm("ab", ("ab0", "ab1"), L, rhs=xT)

                once(pe, "qr_ready", L)
                start_job("qrT", L)
                for i in range(2):
                    for t in range(T):
                        o = i * SEQ + t * 128
                        ins = pe.transpose(pair("qrT")[:, o:o + 128],
                                           qr[:, t, 2 * i:2 * i + 2, :].rearrange("p h n -> p (h n)"), ident[:, :])
                        if i == 0 and t == 0:
                            flush(ins)
                end_job("qrT", ins)

                once(pe, "gla_in_ready", L)
                start_job("AT", L)
                for t in range(T):
                    for h in range(GH):
                        o = (t * GH + h) * 128
                        ins = mm(pair("AT")[:, o:o + 128], ke[:, h // 2, 128 * t:128 * t + 128],
                                 qpad[:, h, 128 * t:128 * t + 128], start=True, stop=True)
                end_job("AT", ins)

                def scores(name, t, nkeys):
                    start_job(name, L)
                    for h in range(MH):
                        o = h * nkeys
                        mm(pair(name)[:, o:o + nkeys], qnT[:, h, 128 * t:128 * t + 128], knT[:, h, 0:nkeys],
                           start=True, stop=False)
                        ins = mm(pair(name)[:, o:o + nkeys], qrT[:, h // 2, 128 * t:128 * t + 128],
                                 krT[:, h % 2, 0:nkeys], start=False, stop=True)
                    end_job(name, ins)

                for n in ("qn", "kn", "qrT", "krT"):
                    wait_read(pe, n, L)
                scores("sc0", 0, 128)

                wait_read(pe, "ktT", L)
                wait_read(pe, "gv", L)

                def increments(name, chunks):
                    start_job(name, L)
                    for c in chunks:
                        p0, t = 64 * (c % 2), c // 2
                        for i in range(2):
                            ins = mm(half(name, c % 2)[:, i * 256:i * 256 + 256], kt[p0:p0 + 64, t, i, :],
                                     vg[p0:p0 + 64, t, i * 256:i * 256 + 256], start=True, stop=True)
                    end_job(name, ins)

                increments("kv0", (0, 1))
                increments("kv2", (2,))
                scores("sc1", 1, SEQ)

                fm("ac", ("ac0", "ac1"), L, rhs=xT)
                tm("gr", ("gr0", "gr1"), L, 512)

                once(pe, "soft0_ready", L)
                once(pe, "soft1_ready", L)
                start_job("pT0", L)
                for h in range(MH):
                    ins = pe.transpose(pair("pT0")[:, h * SEQ:h * SEQ + 128], sc0[:, h, :], ident[:, :])
                    if h == 0:
                        flush(ins)
                    ins = pe.transpose(pair("pT0")[:, h * SEQ + 128:h * SEQ + 256], sc1[:, h, 0:128], ident[:, :])
                end_job("pT0", ins)
                start_job("pT1", L)
                for h in range(MH):
                    ins = pe.transpose(pair("pT1")[:, h * 128:h * 128 + 128], sc1[:, h, 128:256], ident[:, :])
                end_job("pT1", ins)

                wait_read(pe, "AT", L)
                wait_read(pe, "kv2", L)
                start_job("glao", L)
                for t in range(T):
                    for h in range(GH):
                        o = half("glao", t)[:, h * 128:h * 128 + 128]
                        ins = mm(o, ATm[:, t, h, :], vg[:, t, h * 128:h * 128 + 128], start=True, stop=True,
                                 skip_group_check=True)
                        for cc in range(2):
                            c = 2 * t + cc
                            if c:
                                ins = mm(o[64 * cc:64 * cc + 64, :], qpad[:, h, 64 * c:64 * c + 64],
                                         St[:, c - 1, h // 2, (h % 2) * 128:(h % 2) * 128 + 128],
                                         start=False, stop=True, skip_group_check=True)
                end_job("glao", ins)

                fm("ax", ("ax0", "ax1"), L, rhs=xT)

                wait_read(pe, "pT0", L)
                wait_read(pe, "pT1", L)
                wait_read(pe, "vv", L)
                start_job("yc", L)
                for h in range(MH):
                    o = h * SEQ
                    ins = mm(pair("yc")[:, o:o + SEQ], vm[:, 0, h * 128:h * 128 + 128], pT0[:, h, :],
                             start=True, stop=True, skip_group_check=True)
                    if h == 0:
                        flush(ins)
                    ins = mm(pair("yc")[:, o + 128:o + 256], vm[:, 1, h * 128:h * 128 + 128], pT1[:, h, :],
                             start=False, stop=True, skip_group_check=True)
                end_job("yc", ins)

                wait_read(pe, "glao", L)
                start_job("ybT", L)
                for h in range(GH):
                    for t in range(T):
                        o = h * SEQ + t * 128
                        ins = pe.transpose(pair("ybT")[:, o:o + 128], rs[:, t, h, :], ident[:, :])
                end_job("ybT", ins)

                for b in BRANCHES:
                    for h in range(2):
                        fm(f"gate_{b}{h}", (f"gate_{b}{h}0", f"gate_{b}{h}1"), L, rhs=xT)
                        if h == 0 and b == "a":
                            once(pe, "ya_ready", L)
                        elif h == 0:
                            wait_read(pe, {"b": "ybT", "c": "yc"}[b], L)
                        name, un = f"br_{b}{h}", f"wbr_{b}{h}"
                        wait_unit(pe, un, L)
                        start_job(name, L)
                        w = unit(un).rearrange("p (k n) -> p k n", k=4)
                        for m in range(4):
                            for k in range(4):
                                ins = mm(pair(name)[:, m * SEQ:m * SEQ + SEQ], w[:, k, m * 128:m * 128 + 128],
                                         yT[b][:, k, :], start=(k == 0), stop=(k == 3))
                                if m == 0 and k == 0:
                                    flush(ins)
                        end_job(name, ins)
                        pe_release(1)

                def tm_pair(jobs, unit_names, lhsT):
                    for n in jobs:
                        start_job(n, L)
                    last = len(unit_names) - 1
                    whole = range(last - 1)
                    steps = [(i, kk, n) for i in whole for kk in range(2) for n in range(2)]
                    steps += [(i, kk, n) for n in range(2) for i in range(last - 1, last + 1) for kk in range(2)]
                    for i, kk, n in steps:
                        if (kk, n) == (0, 0):
                            wait_unit(pe, unit_names[i], L)
                        w = unit(unit_names[i]).rearrange("p (k n) -> p k n", k=2)
                        k = 2 * i + kk
                        for t in range(T):
                            ins = mm(half(jobs[n], t), lhsT[:, k, 128 * t:128 * t + 128],
                                     w[:, kk, n * 512:n * 512 + 512], start=(k == 0), stop=(k == 2 * last + 1))
                            if (kk, n, t) == (0, 0, 0):
                                flush(ins)
                        if i == last and kk == 1:
                            end_job(jobs[n], ins)
                        if (kk, n) == (1, 1):
                            pe_release(1)

                pe.wait_ge(sig_used, 4 * L + 4)
                tm_pair(("wo0", "wo1"), [f"wo_{i}" for i in range(4)], merged)

                start_job("pTr", L)
                wait_unit(pe, "p", L)
                pin = unit("p")[:, 0:T * PLE].rearrange("p (t n) -> p t n", t=T)
                for i in range(2):
                    for t in range(T):
                        o = i * SEQ + t * 128
                        ins = pe.transpose(pair("pTr")[:, o:o + 128], pin[:, t, i * 128:i * 128 + 128], ident[:, :])
                        if i == 0 and t == 0:
                            flush(ins)
                end_job("pTr", ins)
                pe_release(1)
                wait_read(pe, "pTr", L)

                def ple_up(n):
                    start_job(f"pu{n}", L)
                    if n == 0:
                        wait_unit(pe, "pup", L)
                    w = unit("pup").rearrange("p (k n) -> p k n", k=2)
                    for t in range(T):
                        for k in range(2):
                            ins = mm(half(f"pu{n}", t), pT[:, k, 128 * t:128 * t + 128],
                                     w[:, k, n * 512:n * 512 + 512], start=(k == 0), stop=(k == 1))
                            if n == 0 and k == 0 and t == 0:
                                flush(ins)
                    end_job(f"pu{n}", ins)

                ple_up(0)

                transposes_of_x("x1T_lo", "x1T_hi", 1, L)
                wait_xT(1, L, "logit", IDLE["x1T"])
                for t in range(T):
                    for k in range(K):
                        ins = mm(half("logit", t)[:, 0:NLG], xT[:, k, 128 * t:128 * t + 128], wr[:, k, :],
                                 start=(k == 0), stop=(k == K - 1))
                end_job("logit", ins)
                ple_up(1)
                pe_release(1)
                start_job("rank", L)
                keep_clock(half("rank", 1).rearrange("p (a n) -> p a n", a=4), IDLE["router"])
                once(pe, "asg_ready", L)
                r = half("rank", 0)
                pe_release(1)
                flush(mm(r[:, 0:NE], tri[:, :], asg[:, 0, :], start=True, stop=True))
                mm(r[:, NE:2 * NE], tri[:, :], asg[:, 1, :], start=True, stop=False)
                mm(r[:, NE:2 * NE], ones[:, :], asg[:, 0, :], start=False, stop=True)
                mm(r[:, 2 * NE:3 * NE], ones[:, :], asg[:, 0, :], start=True, stop=False)
                ins = mm(r[:, 2 * NE:3 * NE], ones[:, :], asg[:, 1, :], start=False, stop=True)
                end_job("rank", ins)

                for p in range(4):
                    n = len([j for j in range(JOBS.index("rank") + 1) if j % 4 == p])
                    pe.wait_ge(free[p], L * JOBS_OF[p] + (n + 1))
                keep_clock(ps[:, 0, :].rearrange("p (a n) -> p a n", a=4), IDLE["first P"])
                once(pe, "xp_ready", L)
                once(pe, "yacc_zero", L)
                alone(pe)
                def group(s, pb, p_count, turn, idle=0):
                    def wslot(n):
                        q = MOE0 + n
                        pe.wait_ge(landed[q % RING], turn + (16 * (q // RING + 1) + early(q)))
                        return ring[:, q % RING, :]

                    pe.wait_ge(P_ready, p_count)
                    for k in range(K):
                        for t in range(T):
                            ins = mm(ps[:, k // 4, (k % 4) * 128:(k % 4) * 128 + 128], xp[:, t, k, :],
                                     Psel[pb][:, t, :], start=(t == 0), stop=(t == T - 1))
                    ins.then_inc(gathered, 1)
                    for t in range(T):
                        ins = pe.transpose(ps[:, 3, 256 + 128 * t:384 + 128 * t], Pw[pb][:, t, :], ident[:, :])
                    ins.then_inc(pwt_full, 1)
                    pe.wait_ge(xg_a, s + 1)
                    pe.wait_ge(xg_d, s + 1)
                    for i in range(2):
                        w = [wslot(4 * i + j).rearrange("p (k n) -> p k n", k=K) for j in range(4)]
                        for k in range(K):
                            for j in range(4):
                                ins = mm(ps[32 * j:32 * j + 32, 2, i * 256:i * 256 + 256],
                                         xgT[:, k, 32 * j:32 * j + 32], w[j][:, k, :],
                                         start=(k == 0), stop=(k == K - 1))
                                if i == 1 and k == K - 1 and j == 2:
                                    ins.then_inc(ring_free, 3)
                        if i == 0:
                            ins.then_inc(ring_free, 4)
                    ins.then_inc(h_full, 1)
                    pe.wait_ge(h_ready, s + 1)
                    for c in range(2):
                        ins = pe.transpose(ps[:, 3, 128 * c:128 * c + 128], hperm[:, c, :], ident[:, :])
                        if c == 0:
                            ins.then_inc(ring_free, 1)
                    ins.then_inc(ht_full, 1)
                    pe.wait_ge(acc_done, 2 * s + 1)
                    keep_clock(ps[:, 4, :].rearrange("p (a n) -> p a n", a=4), idle)
                    pe.wait_ge(ht_ready, s + 1)
                    w = [wslot(8 + j).rearrange("p (c n) -> p c n", c=2) for j in range(4)]
                    for n in range(2):
                        for c in range(2):
                            for j in range(4):
                                ins = mm(ps[32 * j:32 * j + 32, 4 + n, :], hT[:, c, 32 * j:32 * j + 32],
                                         w[j][:, c, n * 512:n * 512 + 512], start=(c == 0), stop=(c == 1))
                                if n == 1 and c == 1 and j == 2:
                                    ins.then_inc(ring_free, 3)
                    ins.then_inc(y_full, 1)
                    pe.wait_ge(y_ready, s + 1)
                    pe.wait_ge(pwt_ready, s + 1)
                    for t in range(T):
                        for n in range(2):
                            ins = mm(ps[:, (6 if t == 0 else 4) + n, :], PwT[:, 128 * t:128 * t + 128],
                                     ysb[:, n * 512:n * 512 + 512], start=True, stop=True)
                            if t == 0 and n == 0:
                                ins.then_inc(ring_free, 1)
                        ins.then_inc(c_full, 1)

                with pe.Fori(0, GROUPS // ROUND) as g:
                    for uu in range(ROUND):
                        group(L * ALLG + g * ROUND + uu, uu % 2, L * (ALLG + 1) + g * ROUND + (uu + 1),
                              L * (16 * TURNS) + g * (16 * ROUND) + 16 * uu, idle=IDLE["hidden"] if uu == ROUND - 1 else 0)
                once(pe, "over_ready", L)
                alone(pe)
                n_over = pe.value_load(oe[0:1, OVER:OVER + 1], min_val=0, max_val=OVER)
                with pe.If(n_over > 0):
                    with pe.Fori(0, OVER // 4) as g:
                        group(L * ALLG + g + GROUPS, 1, L * (ALLG + 1) + g + (GROUPS + 2),
                              L * (16 * TURNS) + g * 16 + 16 * GROUPS)
                with pe.Else():
                    pe.drain()
                    for sm, n in ((gathered, 1), (pwt_full, 1), (h_full, 1), (ht_full, 1), (y_full, 1), (c_full, 2),
                                  (ring_free, 12)):
                        pe.sem_inc(sm, n * (ALLG - GROUPS))
                pe.wait_ge(acc_done, 2 * ALLG * L + 2 * ALLG + 1)

                transposes_of_x("x2T_lo", "x2T_hi", 2, L, idle=IDLE["second LayerNorm"])
                wait_xT(2, L, "pg0", IDLE["x2T"])
                tm_pair(("pg0", "pg1"), [f"pgw{i}" for i in range(4)], xT)

        @block.scalar
        def _(act):
            ch = Chain(act, act_chain, ACT_CHAIN)
            link = ch.link

            def done(name, ins):
                ins.then_inc(free[job(name)[0]], 1)

            def copy_out(name, L, dst, src):
                wait_full(act, name, L)
                done(name, act.copy(dst, src))

            act.dma_start(x[:, :, :], a["x"][0].rearrange("(t p) d -> p t d", p=128)).then_inc(pre, 16)
            act.dma_start(unit("ln3"), a["ln0"].rearrange("g d -> (g d)").unsqueeze(0).to_broadcast([128, 2 * D])
                          ).then_inc(landed[unit_pos("ln3") % RING], 16)
            act.dma_start(posi[:, :], a["positions"][0].rearrange("(t p) -> p t", p=128),
                           allow_slow_non_contiguous=True).then_inc(pre, 16)
            act.dma_start(ln0rows, a["ln0"].rearrange("g (k p) -> (g k) p", p=128)).then_inc(pre_vec, 16)
            act.wait_ge(ev["ang_ready"], 1)
            act.activation(sin[:, :, :], sin[:, :, :], ACT.Sin)
            act.activation(cos[:, :, :], cos[:, :, :], ACT.Sin).then_inc(ev["cs_ready"], 1)

            with act.Fori(0, DEPTH) as L:
                ch.base, ch.c = L * ch.per, 0

                def xT_half(name, gb):
                    wait_full(act, name, L)
                    for k in range(4):
                        ins = act.activation(xT[:, k, :], pair(name)[:, k * SEQ:k * SEQ + SEQ], ACT.Identity,
                                             scale=gb[:, k:k + 1], bias=gb[:, K + k:K + k + 1])
                    done(name, ins)

                act.wait_ge(lnT_ready, 1)
                xT_half("xT_lo", lnT)
                wait_read(act, "lat", L)
                for t in range(T):
                    act.activation(junk[:, 3 * t:3 * t + 2, :].rearrange("p a n -> p (a n)"), lat[:, t, 0:QR], ACT.Square, scale=QR ** -0.5,
                                   accum_out=st[:, 2 * t:2 * t + 1])
                    ins = act.activation(junk[:, 3 * t + 2, :], lat[:, t, QR:QR + KVR], ACT.Square, scale=KVR ** -0.5,
                                         accum_out=st[:, 2 * t + 1:2 * t + 2])
                ins.then_inc(ev["lat_squares"], 1)
                wait_full(act, "gqk", L)
                act.mul(qk[:, 0:2, :].rearrange("p a n -> p (a n)"), half("gqk", 0), DK ** -0.5)
                ins = act.copy(qk[:, 2:4, :].rearrange("p a n -> p (a n)"), half("gqk", 1))
                done("gqk", ins)
                once(act, "lat_squares", L)
                copy_out("glr", L, glrT, pair("glr")[0:LR, 0:SEQ])
                once(act, "zabs_ready", L)
                link(act.activation(za, za, ACT.Exp, scale=-1.0))
                act.activation(za, za, ACT.Ln, bias=1.0).then_inc(ev["lnz_ready"], 1)
                wait_read(act, "vecT", L)
                wait_full(act, "latT", L)
                for i in range(2):
                    act.mul(cqT[:, i, :], pair("latT")[:, i * SEQ:i * SEQ + SEQ], vecT[:, 14 + i:15 + i])
                ins = act.mul(ckvT, pair("latT")[:, 2 * SEQ:3 * SEQ], vecT[:, 16:17])
                done("latT", ins)
                copy_out("krT", L, krT.rearrange("p a n -> p (a n)"), pair("krT")[:, 0:512])
                once(act, "bcum_ready", L)
                act.activation(E1, bcum, ACT.Exp, scale=1.0 / TAU)
                act.activation(E2, bcum, ACT.Exp, scale=-1.0 / TAU)
                for i in range(2):
                    for c in range(4):
                        ins = act.activation(E3[:, i, 64 * c:64 * c + 64], bcum[:, i, 64 * c:64 * c + 64], ACT.Exp,
                                             scale=-1.0 / TAU, bias=st[:, 8 + 4 * i + c:9 + 4 * i + c])
                ins.then_inc(ev["exps_ready"], 1)
                copy_out("gv", L, vg.rearrange("p a n -> p (a n)"), pair("gv"))
                copy_out("qn", L, qnT.rearrange("p a n -> p (a n)"), pair("qn"))
                copy_out("kn", L, knT.rearrange("p a n -> p (a n)"), pair("kn"))
                copy_out("ab", L, yaT.rearrange("p a n -> p (a n)"), pair("ab"))
                copy_out("qrT", L, qrT.rearrange("p a n -> p (a n)"), pair("qrT")[:, 0:512])
                for t, sct in ((0, sc0), (1, sc1)):
                    once(act, f"max{t}_ready", L)
                    for h in range(MH):
                        ins = act.activation(sct[:, h, :], sct[:, h, :], ACT.Exp, scale=SCALE,
                                             bias=st[:, 24 + 4 * t + h:25 + 4 * t + h],
                                             accum_out=st[:, 32 + 4 * t + h:33 + 4 * t + h])
                    ins.then_inc(ev[f"exp{t}_ready"], 1)
                copy_out("ac", L, ac.rearrange("p a n -> p (a n)"), pair("ac"))
                wait_full(act, "gr", L)
                ins = act.activation(rs.rearrange("p t h n -> p (t h n)"), pair("gr"), ACT.Silu)
                done("gr", ins)
                copy_out("pT0", L, pT0.rearrange("p a n -> p (a n)"), pair("pT0"))
                copy_out("pT1", L, pT1.rearrange("p a n -> p (a n)"), pair("pT1")[:, 0:512])
                wait_full(act, "glao", L)
                for t in range(T):
                    for h in range(GH):
                        i = 40 + 4 * t + h
                        ins = act.activation(junk[:, 4 * t + h, :], half("glao", t)[:, h * 128:h * 128 + 128], ACT.Square,
                                             scale=DV ** -0.5, accum_out=st[:, i:i + 1])
                ins.then_inc(ev["o_squares"], 1)
                copy_out("yc", L, ycT.rearrange("p a n -> p (a n)"), pair("yc"))
                copy_out("ybT", L, ybT.rearrange("p a n -> p (a n)"), pair("ybT"))
                n = 0
                once(act, "ya_ready", L)
                for b in BRANCHES:
                    for h in range(2):
                        name = f"gate_{b}{h}"
                        wait_full(act, name, L)
                        if n in (2, 3):
                            wait_read(act, f"br_{BRANCHES[0]}{n - 2}", L)
                        elif n > 3:
                            act.wait_ge(sig_used, 4 * L + (n - 3))
                        done(name, act.activation(sig[n % 2].rearrange("p a n -> p (a n)"), pair(name), ACT.Sigmoid))
                        n += 1
                copy_out("pTr", L, pT.rearrange("p a n -> p (a n)"), pair("pTr")[:, 0:512])
                copy_out("pu0", L, pus[:, 0, :, :].rearrange("p t n -> p (t n)"), pair("pu0"))
                xT_half("x1T_lo", vecT[:, 17:33])
                act.wait_ge(xfinal, 3 * L + 2)
                for t in range(T):
                    ins = act.copy(xp[:, t, :, :], x[:, t, :].rearrange("p (q k) -> p k q", k=K))
                ins.then_inc(ev["xp_ready"], 1)
                copy_out("pu1", L, pus[:, 1, :, :].rearrange("p t n -> p (t n)"), pair("pu1"))
                once(act, "gmax_ready", L)
                for t in range(T):
                    ins = act.activation(rt[:, t, 40:48], lg[:, t, 0:NG], ACT.Exp, bias=rt[:, t, 16:17],
                                         accum_out=rt[:, t, 17:18])
                ins.then_inc(ev["gexp_ready"], 1)
                once(act, "dtop_ready", L)
                act.activation(rt[:, :, 19:20], rt[:, :, 18:19], ACT.Exp).then_inc(ev["etop_ready"], 1)

                def group(s):
                    act.wait_ge(gathered, s + 1)
                    act.copy(xgT[:, 0:4, :].rearrange("p k n -> p (k n)"), ps[:, 0, :]).then_inc(xg_a, 1)
                    act.wait_ge(h_full, s + 1)
                    act.activation(silu, ps[:, 2, 0:256], ACT.Silu).then_inc(silu_ready, 1)
                    act.wait_ge(ht_full, s + 1)
                    act.copy(hT.rearrange("p c n -> p (c n)"), ps[:, 3, 0:256]).then_inc(ht_ready, 1)
                    act.wait_ge(y_full, s + 1)
                    act.copy(ysb, ps[:, 4:6, :].rearrange("p a n -> p (a n)")).then_inc(y_ready, 1)

                with act.Fori(0, GROUPS) as g:
                    group(L * ALLG + g)
                once(act, "over_ready", L)
                alone(act)
                n_over = act.value_load(oe[0:1, OVER:OVER + 1], min_val=0, max_val=OVER)
                with act.If(n_over > 0):
                    with act.Fori(0, OVER // 4) as g:
                        group(L * ALLG + g + GROUPS)
                with act.Else():
                    act.drain()
                    for sm in (xg_a, silu_ready, ht_ready, y_ready):
                        act.sem_inc(sm, ALLG - GROUPS)
                xT_half("x2T_lo", vecT[:, 33:49])
                for n in range(2):
                    wait_read(act, f"pg{n}", L)
                    act.activation(pgs[:, n, :, :], pgs[:, n, :, :], ACT.Sigmoid).then_inc(pgs_sig, 1)
                ch.check(1)

        @block.vector
        def _(dve):
            ch = Chain(dve, dve_chain, DVE_CHAIN)
            link = ch.link

            def done(name, ins):
                ins.then_inc(free[job(name)[0]], 1)

            def signal(name, ins):
                ins.then_inc(ev[name], 1)

            def ln_stats(h):
                for t in range(T):
                    ins = dve.bn_stats(st6[:, t, h, :], x[:, t, 512 * h:512 * h + 512])
                link(ins)

            def layer_norm(powers):
                alone(dve)
                for t in range(T):
                    ins = dve.bn_aggr(mv[:, t, :], st6[:, t, :, :])
                ins.then_inc(power_in, 1)
                dve.wait_ge(power_out, powers)
                for t in range(T):
                    ins = dve.tensor_scalar(x[:, t, :], x[:, t, :], mv[:, t, 0:1], rstd[:, t:t + 1],
                                            ALU.subtract, ALU.mult)
                ins.then_inc(x_ready, 1)

            def gain_and_bias(v, n):
                for t in range(T):
                    ins = dve.tensor_tensor(x[:, t, :], x[:, t, :], v[:, 0, :], ALU.mult)
                link(ins)
                for t in range(T):
                    ins = dve.tensor_tensor(x[:, t, :], x[:, t, :], v[:, 1, :], ALU.add)
                ins.then_inc(xfinal, 1)
                dve.wait_ge(xfinal, n)

            dve.wait_ge(pre, 32)
            for h in range(2):
                ln_stats(h)
            layer_norm(1)
            dve.wait_ge(ln0_full, 1)
            dve.tensor_copy(lnT[:, :], ps[:, 6, 0:16]).then_inc(lnT_ready, 1)
            dve.wait_ge(inv_ready, 1)
            link(dve.tensor_copy(posf[:, :], posi[:, :]))
            for t in range(T):
                ins = dve.tensor_scalar(sin[:, t, :], inv[:, :], posf[:, t:t + 1], None, ALU.mult)
            link(ins)
            link(dve.tensor_scalar(cos[:, :, :], sin[:, :, :], float(1 / (2 * np.pi)), 12582912.0, ALU.mult, ALU.add))
            link(dve.tensor_scalar(cos[:, :, :], cos[:, :, :], 12582912.0, None, ALU.subtract))
            c1 = 6.28125
            c2 = float(np.float32(np.round((2 * np.pi - c1) * 2 ** 21) / 2 ** 21))
            c3 = float(2 * np.pi - c1 - c2)
            for c in (c1, c2, c3):
                link(dve.scalar_tensor_tensor(sin[:, :, :], cos[:, :, :], -c, sin[:, :, :], ALU.mult, ALU.add))
            pi = float(np.nextafter(np.float32(np.pi), np.float32(0)))
            link(dve.tensor_scalar(sin[:, :, :], sin[:, :, :], pi, -pi, ALU.min, ALU.max))
            link(dve.tensor_scalar(cos[:, :, :], sin[:, :, :], -1.0, None, ALU.mult))
            link(dve.tensor_tensor(cos[:, :, :], cos[:, :, :], sin[:, :, :], ALU.max))
            ins = dve.tensor_scalar(cos[:, :, :], cos[:, :, :], -1.0, float(np.pi / 2), ALU.mult, ALU.add)
            signal("ang_ready", ins)
            link(dve.memset(u[:, :, 0:2], 0.0))
            ch.check(0)
            total0 = ch.c

            with dve.Fori(0, DEPTH) as L:
                ch.base, ch.c = L * ch.per + total0, 0

                def xT_half(name, gb):
                    wait_full(dve, name, L)
                    for k in range(4, K):
                        ins = dve.tensor_scalar(xT[:, k, :], pair(name)[:, (k - 4) * SEQ:(k - 3) * SEQ],
                                                gb[:, k:k + 1], gb[:, K + k:K + k + 1], ALU.mult, ALU.add)
                    done(name, ins)

                xT_half("xT_hi", lnT)
                dve.wait_ge(landed[unit_pos("ln3") % RING], L * (16 * TURNS) + 16)
                gain_and_bias(unit("ln3").rearrange("p (g d) -> p g d", g=2), 3 * L + 1)
                wait_full(dve, "lat", L)
                for t in range(T):
                    ins = dve.tensor_copy(lat[:, t, :], half("lat", t)[:, 0:LAT])
                done("lat", ins)
                wait_read(dve, "lat", L)
                dve.wait_ge(ev["cs_ready"], 1)
                dve.wait_ge(consts, 1)
                kx1, kx2 = lat[:, :, QR + KVR:QR + KVR + 32], lat[:, :, QR + KVR + 32:LAT]
                m = [r_[:, :, 0, :] for r_ in rope_tmp]
                dve.tensor_tensor(m[0], kx1, cos[:, :, :], ALU.mult)
                dve.tensor_tensor(m[1], kx2, sin[:, :, :], ALU.mult)
                dve.tensor_tensor(m[2], kx1, sin[:, :, :], ALU.mult)
                link(dve.tensor_tensor(m[3], kx2, cos[:, :, :], ALU.mult))
                for i in range(2):
                    dve.tensor_tensor(krp[:, :, i, 64 * i:64 * i + 32], m[0], m[1], ALU.subtract)
                    ins = dve.tensor_tensor(krp[:, :, i, 64 * i + 32:64 * i + 64], m[2], m[3], ALU.add)
                signal("kr_ready", ins)
                dve.wait_ge(power_out, 5 * L + 2)
                for t in range(T):
                    dve.tensor_scalar(lat[:, t, 0:QR], lat[:, t, 0:QR], st[:, 4 + 2 * t:5 + 2 * t], None, ALU.mult)
                    ins = dve.tensor_scalar(lat[:, t, QR:QR + KVR], lat[:, t, QR:QR + KVR],
                                            st[:, 5 + 2 * t:6 + 2 * t], None, ALU.mult)
                signal("lat_normed", ins)
                wait_full(dve, "vecT", L)
                done("vecT", dve.tensor_copy(vecT[:, :], pair("vecT")[:, 0:65]))
                wait_read(dve, "vecT", L)
                wait_full(dve, "z", L)
                for i in range(2):
                    ins = dve.tensor_scalar(zb[:, i, :], pair("z")[:, i * SEQ:i * SEQ + SEQ], vecT[:, 12 + i:13 + i],
                                            None, ALU.add)
                done("z", ins)
                wait_read(dve, "z", L)
                link(dve.tensor_scalar(za, zb, -1.0, None, ALU.mult))
                ins = dve.tensor_tensor(za, za, zb, ALU.max)
                signal("zabs_ready", ins)
                once(dve, "lnz_ready", L)
                link(dve.scalar_tensor_tensor(zb, zb, 0.0, za, ALU.min, ALU.subtract))
                for i in range(2):
                    for c in range(4):
                        o = slice(64 * c, 64 * c + 64)
                        ins = dve.tensor_tensor_scan(bcum[:, i, o], ones[:, 0:64], zb[:, i, o], 0.0, ALU.mult, ALU.add)
                link(ins)
                last = bcum.rearrange("p i (c n) -> p i c n", c=4)[:, :, :, 63]
                ins = dve.tensor_scalar(st[:, 8:16].rearrange("p (i c) -> p i c", i=2), last, 1.0 / TAU, None, ALU.mult)
                signal("bcum_ready", ins)
                once(dve, "exps_ready", L)
                wait_read(dve, "gqk", L)
                ins = dve.tensor_tensor(ktF, qk[:, 2:4, :], E3, ALU.mult)
                signal("ktF_ready", ins)
                dve.tensor_tensor(ke, qk[:, 2:4, :], E2, ALU.mult)
                for h in range(GH):
                    o = slice(64 * (h % 2), 64 * (h % 2) + 64)
                    ins = dve.tensor_tensor(qpad[o, h, :], qk[o, h // 2, :], E1[o, h // 2, :], ALU.mult)
                signal("gla_in_ready", ins)
                wait_full(dve, "qr", L)
                qv = ps[:, bank(job("qr")[0]):bank(job("qr")[0]) + 2, 0:MH * ROPE].rearrange("p t (h n) -> p t h n", h=MH)
                for t in range(T):
                    q1, q2 = qv[:, t, :, 0:32], qv[:, t, :, 32:64]
                    cb = cos[:, t, :].unsqueeze(1).to_broadcast([128, MH, 32])
                    sbb = sin[:, t, :].unsqueeze(1).to_broadcast([128, MH, 32])
                    dve.tensor_tensor(rope_tmp[0][:, t, :, :], q1, cb, ALU.mult)
                    dve.tensor_tensor(rope_tmp[1][:, t, :, :], q2, sbb, ALU.mult)
                    dve.tensor_tensor(rope_tmp[2][:, t, :, :], q1, sbb, ALU.mult)
                    ins = dve.tensor_tensor(rope_tmp[3][:, t, :, :], q2, cb, ALU.mult)
                done("qr", ins)
                wait_read(dve, "qr", L)
                dve.tensor_tensor(qr[:, :, :, 0:32], rope_tmp[0], rope_tmp[1], ALU.subtract)
                ins = dve.tensor_tensor(qr[:, :, :, 32:64], rope_tmp[2], rope_tmp[3], ALU.add)
                signal("qr_ready", ins)
                wait_full(dve, "vv", L)
                ins = dve.tensor_copy(vm.rearrange("p a n -> p (a n)"), pair("vv"))
                done("vv", ins)
                wait_full(dve, "ktT", L)
                ins = dve.tensor_copy(kt.rearrange("p t i n -> p (t i n)"), pair("ktT")[:, 0:512])
                done("ktT", ins)
                wait_full(dve, "AT", L)
                alone(dve)
                ins = dve.copy_predicated(ATm.rearrange("p t h n -> p (t h) n"),
                                          gmask[:, :].unsqueeze(1).to_broadcast([128, T * GH, 128]),
                                          pair("AT").rearrange("p (a n) -> p a n", n=128))
                done("AT", ins)

                def mask_and_max(t, name, sct, n):
                    wait_full(dve, name, L)
                    src = pair(name)[:, 0:MH * n].rearrange("p (h n) -> p h n", h=MH)
                    if t == 1:
                        dve.tensor_copy(sct[:, :, 0:128], src[:, :, 0:128])
                    ins = dve.tensor_tensor(sct[:, :, n - 128:n], src[:, :, n - 128:n],
                                            smask[:, :].unsqueeze(1).to_broadcast([128, MH, 128]), ALU.add)
                    done(name, ins)
                    wait_read(dve, name, L)
                    link(dve.tensor_reduce(st[:, 16 + 4 * t:20 + 4 * t], sct, AX.X, ALU.max))
                    ins = dve.tensor_scalar(st[:, 24 + 4 * t:28 + 4 * t], st[:, 16 + 4 * t:20 + 4 * t], -SCALE, None, ALU.mult)
                    signal(f"max{t}_ready", ins)

                def normalise(t, sct, n):
                    once(dve, f"exp{t}_ready", L)
                    link(dve.reciprocal(st[:, 48 + 4 * t:52 + 4 * t], st[:, 32 + 4 * t:36 + 4 * t]))
                    for h in range(MH):
                        ins = dve.tensor_scalar(sct[:, h, :], sct[:, h, :], st[:, 48 + 4 * t + h:49 + 4 * t + h], None, ALU.mult)
                    signal(f"soft{t}_ready", ins)

                wait_read(dve, "qrT", L)
                mask_and_max(0, "sc0", sc0, 128)
                kvp = [half("kv0", 0), half("kv0", 1), half("kv2", 0)]
                wait_full(dve, "kv0", L)
                link(dve.tensor_copy(St[:, 0, :, :].rearrange("p i n -> p (i n)"), kvp[0]))
                for c in (1, 2):
                    if c == 2:
                        wait_full(dve, "kv2", L)
                    for i in range(2):
                        ins = dve.scalar_tensor_tensor(St[:, c, i, :], St[:, c - 1, i, :],
                                                       E1[:, i, 64 * c + 63:64 * c + 64],
                                                       kvp[c][:, i * 256:i * 256 + 256], ALU.mult, ALU.add)
                    if c == 1:
                        done("kv0", ins)
                        wait_read(dve, "kv0", L)
                    else:
                        done("kv2", ins)
                normalise(0, sc0, 128)
                mask_and_max(1, "sc1", sc1, SEQ)
                normalise(1, sc1, SEQ)
                wait_read(dve, "gr", L)
                link(dve.tensor_tensor(rs.rearrange("p t h n -> p (t h) n"), rs.rearrange("p t h n -> p (t h) n"),
                                       gnorm[:, :].unsqueeze(1).to_broadcast([128, T * GH, DV]), ALU.mult))
                dve.wait_ge(power_out, 5 * L + 3)
                wait_full(dve, "glao", L)
                for t in range(T):
                    for h in range(GH):
                        ins = dve.scalar_tensor_tensor(rs[:, t, h, :], half("glao", t)[:, h * 128:h * 128 + 128],
                                                       st[:, 40 + 4 * t + h:41 + 4 * t + h], rs[:, t, h, :],
                                                       ALU.mult, ALU.mult)
                done("glao", ins)
                wait_read(dve, "ac", L)
                wait_full(dve, "ax", L)
                ins = dve.tensor_tensor(u[:, :, 2:SEQ + 2], ac, pair("ax").rearrange("p (a n) -> p a n", a=4), ALU.mult)
                done("ax", ins)
                wait_read(dve, "ax", L)
                for i in range(4):
                    ins = dve.tensor_scalar(ac[:, i, :], u[:, i, 2:SEQ + 2], vecT[:, 8 + i:9 + i], None, ALU.mult)
                link(ins)
                for tap in (1, 0):
                    for i in range(4):
                        ins = dve.scalar_tensor_tensor(ac[:, i, :], u[:, i, tap:SEQ + tap],
                                                       vecT[:, 4 * tap + i:4 * tap + i + 1], ac[:, i, :],
                                                       ALU.mult, ALU.add)
                    link(ins)
                wait_read(dve, "ab", L)
                signal("ya_ready", dve.tensor_tensor(yaT, yaT, ac, ALU.mult))
                n = 0
                for b in BRANCHES:
                    for h in range(2):
                        name = f"br_{b}{h}"
                        wait_read(dve, f"gate_{b}{h}", L)
                        wait_full(dve, name, L)
                        src = pair(name).rearrange("p (a n) -> p a n", a=4)
                        dst = merged[:, 4 * h:4 * h + 4, :]
                        if n < 2:
                            done(name, dve.tensor_tensor(dst, sig[n % 2], src, ALU.mult))
                        else:
                            ins = dve.tensor_tensor(sig[n % 2], sig[n % 2], src, ALU.mult)
                            done(name, ins)
                            wait_read(dve, name, L)
                            dve.tensor_tensor(dst, dst, sig[n % 2], ALU.add).then_inc(sig_used, 1)
                            dve.wait_ge(sig_used, 4 * L + (n - 1))
                        n += 1

                def residual(names):
                    for h, name in enumerate(names):
                        wait_full(dve, name, L)
                        for t in range(T):
                            o = slice(512 * h, 512 * h + 512)
                            ins = dve.scalar_tensor_tensor(x[:, t, o], x[:, t, o], ALPHA, half(name, t),
                                                           ALU.mult, ALU.add)
                        done(name, ins)
                        wait_read(dve, name, L)
                        ln_stats(h)

                residual(("wo0", "wo1"))
                layer_norm(5 * L + 4)
                xT_half("x1T_hi", vecT[:, 17:33])
                wait_unit(dve, "ln1", L)
                gain_and_bias(unit("ln1").rearrange("p (g d) -> p g d", g=2), 3 * L + 2)
                wait_full(dve, "logit", L)
                for t in range(T):
                    ins = dve.tensor_tensor(lg[:, t, :], half("logit", t)[:, 0:NLG], br[:, :], ALU.add)
                done("logit", ins)
                wait_read(dve, "logit", L)
                alone(dve)
                for t in range(T):
                    ins = dve.max(rt[:, t, 0:8], lg[:, t, 0:NG])
                link(ins)
                for t in range(T):
                    dve.tensor_scalar(rt[:, t, 16:17], rt[:, t, 0:1], -1.0, None, ALU.mult)
                    ins = dve.max_index(idx[:, t, :], rt[:, t, 0:8], lg[:, t, 0:NG])
                signal("gmax_ready", ins)
                once(dve, "gmax_ready", L)
                link(dve.tensor_copy(rt[:, :, 20:21], idx[:, 0:2, 0:1]))
                for t in range(T):
                    ins = dve.tensor_scalar(rt[:, t, 32:40], iota[:, 0:NG], rt[:, t, 20:21], None, ALU.is_equal)
                link(ins)
                for t in range(T):
                    o = big[0].rearrange("p a b -> p (a b)")[:, 64 * t:64 * t + 64].rearrange("p (e g) -> p e g", e=EPG)
                    ins = dve.tensor_tensor(o, lg[:, t, NG:NLG].rearrange("p (g e) -> p e g", e=EPG),
                                            rt[:, t, 32:40].unsqueeze(1).to_broadcast([128, EPG, NG]), ALU.mult)
                link(ins)
                link(dve.tensor_reduce(rt[:, :, 48:56], big[0].rearrange("p a b -> p (a b)")[:, 0:128]
                                       .rearrange("p (t e g) -> p t e g", t=2, e=EPG), AX.X, ALU.add))
                alone(dve)
                for t in range(T):
                    ins = dve.max(rt[:, t, 8:16], rt[:, t, 48:56])
                link(ins)
                alone(dve)
                for t in range(T):
                    ins = dve.max_index(idx[:, 2 + t, :], rt[:, t, 8:16], rt[:, t, 48:56])
                signal("dtop_ready", dve.tensor_tensor(rt[:, :, 18:19], rt[:, :, 9:10], rt[:, :, 8:9], ALU.subtract))
                once(dve, "dtop_ready", L)
                link(dve.tensor_copy(rt[:, :, 21:23], idx[:, 2:4, 0:2]))
                for i in range(2):
                    ins = dve.scalar_tensor_tensor(rt[:, :, 25 + i:26 + i], rt[:, :, 20:21], float(EPG),
                                                   rt[:, :, 21 + i:22 + i], ALU.mult, ALU.add)
                link(ins)
                for t in range(T):
                    ins = dve.tensor_scalar(asg[:, t, :], iota[:, :], rt[:, t, 25:26], None, ALU.is_equal)
                link(ins)
                for t in range(T):
                    ins = dve.scalar_tensor_tensor(asg[:, t, :], iota[:, :], rt[:, t, 26:27], asg[:, t, :],
                                                   ALU.is_equal, ALU.add)
                signal("asg_ready", ins)
                once(dve, "etop_ready", L)
                once(dve, "gexp_ready", L)
                link(dve.scalar_tensor_tensor(rt[:, :, 23:24], rt[:, :, 19:20], 1.0, rt[:, :, 17:18], ALU.add, ALU.mult))
                link(dve.reciprocal(rt[:, :, 23:24], rt[:, :, 23:24]))
                link(dve.tensor_tensor(rt[:, :, 24:25], rt[:, :, 23:24], rt[:, :, 19:20], ALU.mult))
                for t in range(T):
                    dve.tensor_scalar(wx[:, t, 0:NE], iota[:, :], rt[:, t, 25:26], rt[:, t, 23:24], ALU.is_equal, ALU.mult)
                    ins = dve.tensor_scalar(big[0][:, t, :], iota[:, :], rt[:, t, 26:27], rt[:, t, 24:25],
                                            ALU.is_equal, ALU.mult)
                link(ins)
                link(dve.tensor_tensor(wx[:, :, 0:NE], wx[:, :, 0:NE], big[0][:, 0:2, :], ALU.add))
                wait_full(dve, "rank", L)
                rk = half("rank", 0)
                dve.scalar_tensor_tensor(rankx[:, :, 0:NE], rk[:, 0:2 * NE].rearrange("p (t e) -> p t e", t=2), 1.0,
                                         asg, ALU.add, ALU.mult)
                ins = dve.tensor_copy(cnt, rk[:, 2 * NE:3 * NE])
                done("rank", ins)
                wait_read(dve, "rank", L)
                dve.memset(rankx[:, :, NE + OVER:NR], -1.0)
                dve.memset(wx[:, :, NE + OVER:NR], 0.0)
                link(dve.tensor_scalar(rankx[:, :, 0:NE], rankx[:, :, 0:NE], 1.0, None, ALU.subtract))

                def build_P(col, pb):
                    iota_b = iota[:, 0:32].unsqueeze(1).to_broadcast([128, 4, 32])
                    for t in range(T):
                        o = Psel[pb][:, t, :].rearrange("p (j r) -> p j r", j=4)
                        ins = dve.tensor_tensor(o, rankx[:, t, col].unsqueeze(2).to_broadcast([128, 4, 32]), iota_b,
                                                ALU.is_equal)
                    link(ins)
                    for t in range(T):
                        ins = dve.tensor_tensor(Pw[pb][:, t, :].rearrange("p (j r) -> p j r", j=4),
                                                Psel[pb][:, t, :].rearrange("p (j r) -> p j r", j=4),
                                                wx[:, t, col].unsqueeze(2).to_broadcast([128, 4, 32]), ALU.mult)
                    ins.then_inc(P_ready, 1)

                build_P(slice(0, 4), 0)
                o7 = big[0].rearrange("p a b -> p (a b)")[:, 0:NE * 7].rearrange("p (e m) -> p e m", m=7)
                link(dve.tensor_tensor(o7, cnt.unsqueeze(2).to_broadcast([128, NE, 7]),
                                       iota32m[:, :].unsqueeze(1).to_broadcast([128, NE, 7]), ALU.is_gt))
                link(dve.tensor_reduce(nov, o7, AX.X, ALU.add))
                link(dve.tensor_reduce(cum[:, 0:1], nov, AX.X, ALU.add))
                signal("over_ready", dve.tensor_copy(oe[:, OVER:OVER + 1], cum[:, 0:1]))

                def table():
                    i16 = iota[:, 0:OVER].unsqueeze(2).to_broadcast([128, OVER, NE])

                    def over_e(ap):
                        return ap.unsqueeze(1).to_broadcast([128, OVER, NE])

                    link(dve.tensor_tensor_scan(cum, ones[:, 0:NE], nov, 0.0, ALU.mult, ALU.add))
                    link(dve.tensor_tensor(big[0], over_e(cum), i16, ALU.is_le))
                    dve.tensor_reduce(ov[:, 0, :], big[0], AX.X, ALU.add)
                    link(dve.tensor_tensor(big[1], big[0], over_e(nov), ALU.mult))
                    link(dve.tensor_reduce(ov[:, 1, :], big[1], AX.X, ALU.add))
                    link(dve.tensor_tensor(ov[:, 2, :], iota[:, 0:OVER], ov[:, 1, :], ALU.subtract))
                    link(dve.tensor_scalar(ov[:, 2, :], ov[:, 2, :], 1.0, 32.0, ALU.add, ALU.mult))
                    signal("table_ready", dve.tensor_scalar(oe[:, 0:OVER], ov[:, 0, :], float(NE - 1), None, ALU.min))
                    link(dve.tensor_tensor(big[0], over_e(iota[:, :]),
                                           ov[:, 0, :].unsqueeze(2).to_broadcast([128, OVER, NE]), ALU.is_equal))
                    for t in range(T):
                        dve.tensor_tensor(big[1], big[0], over_e(rankx[:, t, 0:NE]), ALU.mult)
                        link(dve.tensor_tensor(big[2], big[0], over_e(wx[:, t, 0:NE]), ALU.mult))
                        dve.tensor_reduce(rankx[:, t, NE:NE + OVER], big[1], AX.X, ALU.add)
                        link(dve.tensor_reduce(wx[:, t, NE:NE + OVER], big[2], AX.X, ALU.add))
                        link(dve.tensor_tensor(rankx[:, t, NE:NE + OVER], rankx[:, t, NE:NE + OVER], ov[:, 2, :],
                                               ALU.subtract))

                alone(dve)
                c_before = ch.c
                b_before = ch.base

                def group(s, next_P):
                    dve.wait_ge(gathered, s + 1)
                    dve.tensor_copy(xgT[:, 4:8, :].rearrange("p k n -> p (k n)"), ps[:, 1, :]).then_inc(xg_d, 1)
                    dve.wait_ge(pwt_full, s + 1)
                    dve.tensor_copy(PwT, ps[:, 3, 256:512]).then_inc(pwt_ready, 1)
                    dve.wait_ge(silu_ready, s + 1)
                    dve.tensor_tensor(hperm.rearrange("p c q -> p q c"), silu.rearrange("p (q c) -> p q c", c=2),
                                      ps[:, 2, 256:512].rearrange("p (q c) -> p q c", c=2), ALU.mult).then_inc(h_ready, 1)
                    next_P()
                    for t in range(T):
                        dve.wait_ge(c_full, 2 * s + (t + 1))
                        b = 6 if t == 0 else 4
                        dve.tensor_tensor(yacc[:, t, :], yacc[:, t, :], ps[:, b:b + 2, :].rearrange("p a n -> p (a n)"),
                                          ALU.add).then_inc(acc_done, 1)

                with dve.Fori(0, GROUPS // ROUND) as g:
                    ch.base, ch.c = b_before + g * ch.exp[2] + c_before, 0
                    for uu in range(ROUND):
                        group(L * ALLG + g * ROUND + uu,
                              lambda: build_P(bass.ds(g * (4 * ROUND) + 4 * (uu + 1), 4), (uu + 1) % 2))
                    ch.check(2)
                rounds = (GROUPS // ROUND) * ch.exp[2]
                n_over = dve.value_load(oe[0:1, OVER:OVER + 1], min_val=0, max_val=OVER)
                with dve.If(n_over > 0):
                    ch.base, ch.c = b_before + (c_before + rounds), 0
                    table()
                    alone(dve)
                    ch.check(4)
                    with dve.Fori(0, OVER // 4) as g:
                        ch.base, ch.c = b_before + g * ch.exp[3] + (c_before + rounds + ch.exp[4]), 0
                        build_P(bass.ds(g * 4 + NE, 4), 1)
                        group(L * ALLG + g + GROUPS, lambda: None)
                        ch.check(3)
                with dve.Else():
                    dve.drain()
                    for sm, n in ((P_ready, 1), (xg_d, 1), (pwt_ready, 1), (h_ready, 1), (acc_done, 2),
                                  (dve_chain, ch.exp[3])):
                        dve.sem_inc(sm, n * (ALLG - GROUPS))
                    dve.sem_inc(dve_chain, ch.exp[4])
                    dve.sem_inc(ev["table_ready"], 1)
                ch.base, ch.c = b_before + rounds + (ALLG - GROUPS) * ch.exp[3] + ch.exp[4], c_before
                dve.wait_ge(acc_done, 2 * ALLG * L + 2 * ALLG + 1)
                for t in range(T):
                    ins = dve.scalar_tensor_tensor(x[:, t, :], x[:, t, :], ALPHA, yacc[:, t, :], ALU.mult, ALU.add)
                link(ins)
                for h in range(2):
                    ln_stats(h)
                layer_norm(5 * L + 5)
                xT_half("x2T_hi", vecT[:, 33:49])
                wait_unit(dve, "ln2", L)
                gain_and_bias(unit("ln2").rearrange("p (g d) -> p g d", g=2), 3 * L + 3)
                wait_unit(dve, "bple", L)
                wait_read(dve, "pu1", L)
                for n in range(2):
                    o = slice(512 * n, 512 * n + 512)
                    wait_full(dve, f"pg{n}", L)
                    for t in range(T):
                        ins = dve.tensor_tensor(pgs[:, n, t, :], half(f"pg{n}", t), unit("bple")[:, o], ALU.add)
                    done(f"pg{n}", ins)
                    dve.wait_ge(pgs_sig, 2 * L + (n + 1))
                    link(dve.tensor_tensor(pgs[:, n, :, :], pgs[:, n, :, :], pus[:, n, :, :], ALU.mult))
                    for t in range(T):
                        ins = dve.scalar_tensor_tensor(x[:, t, o], x[:, t, o], ALPHA, pgs[:, n, t, :], ALU.mult, ALU.add)
                    link(ins)
                    ln_stats(n)
                dve.tensor_copy(lnT[:, :], vecT[:, 49:65])
                layer_norm(5 * L + 6)
                ch.check(1)
            ch.base, ch.c = ch.per * DEPTH + total0, 0
            dve.wait_ge(x_ready, 3 * DEPTH + 2)
            dve.wait_ge(landed[unit_pos("ln3") % RING], DEPTH * (16 * TURNS) + 16)
            gain_and_bias(unit("ln3").rearrange("p (g d) -> p g d", g=2), 3 * DEPTH + 1)


def kernel(**inputs):
    import concourse.bacc as bacc
    from concourse.bass_utils import run_bass_kernel_spmd

    arr = {k: np.ascontiguousarray(v) for k, v in inputs.items()}
    lay = {
        "x": arr["x"], "positions": arr["positions"],
        "p": arr["p"].reshape(DEPTH, SEQ, PLE),
        "ln0": np.stack([arr["ln0_g"], arr["ln0_b"]]),
        "w_exp": arr["w_exp"].reshape(DEPTH, D, NE), "b_exp": arr["b_exp"].reshape(DEPTH, NE),
        "w_gate": arr["w_gate"].reshape(DEPTH * NE, D, HID), "w_up": arr["w_up"].reshape(DEPTH * NE, D, HID),
        "w_down": arr["w_down"].reshape(DEPTH * NE, HID, D),
    }
    for i in (1, 2, 3):
        lay[f"ln{i}"] = np.stack([arr[f"ln{i}_g"], arr[f"ln{i}_b"]], axis=1)
    for n in ("w_in", "w_conv", "w_gla_gate", "b_gla_gate", "gla_norm_g", "mla_q_norm_g", "mla_kv_norm_g", "w_uq",
              "w_ukv", "w_br", "w_o", "w_grp", "b_grp", "w_ple_gate", "b_ple_gate", "w_ple_up"):
        lay[n] = arr[n]
    nc = bacc.Bacc("TRN2", target_bir_lowering=False, num_devices=1)
    aps = {n: nc.dram_tensor(f"in_{n}", v.shape, mybir.dt.from_np(v.dtype), kind="ExternalInput").ap()
           for n, v in lay.items()}
    aps["out"] = nc.dram_tensor("out", (1, SEQ, D), F32, kind="ExternalOutput").ap()
    build(nc, aps)
    r = run_bass_kernel_spmd(nc, [{f"in_{n}": v for n, v in lay.items()}], core_ids=[0])
    return r.results[0]["out"]
```
